# Optimizing a Trainium2 kernel written in Bass

```python
import math
import jax, jax.numpy as jnp
from jax import lax
import numpy as np

D_MODEL = 1024
BATCH = 1
SEQ = 512
DEPTH = 2

GDN_HEADS = 4
GDN_HEAD_DIM = 128
CONV_WIDTH = 4
GDN_CHUNK = 64
DIFF_HEADS = 4
DIFF_QK_DIM = 64
DIFF_V_DIM = 2 * DIFF_QK_DIM
FOX_HEADS = 8
FOX_HEAD_DIM = D_MODEL // FOX_HEADS
D_FF = 4 * D_MODEL
PLE_DIM = 256
ROPE_THETA = 10000.0
Q_BLOCK = 128
EPS = 1e-6
NEG_INF = -1e30

N_EVEN = (DEPTH + 1) // 2
N_ODD = DEPTH // 2

GDN_QK = GDN_HEADS * GDN_HEAD_DIM
GDN_V = GDN_HEADS * GDN_HEAD_DIM
DIFF_Q = DIFF_HEADS * 2 * DIFF_QK_DIM
DIFF_V = DIFF_HEADS * DIFF_V_DIM
EVEN_SPLITS = [3 * GDN_QK, GDN_V, GDN_HEADS, GDN_HEADS, DIFF_Q, DIFF_Q, DIFF_V]
EVEN_IN = sum(EVEN_SPLITS)
EVEN_MIX = GDN_V + DIFF_V
ODD_MIX = FOX_HEADS * FOX_HEAD_DIM
ODD_SPLITS = [ODD_MIX, ODD_MIX, ODD_MIX, ODD_MIX, FOX_HEADS]
ODD_IN = sum(ODD_SPLITS)


def split_cols(t, sizes):
    offs = np.concatenate([[0], np.cumsum(sizes)]).tolist()
    return [t[..., offs[i]:offs[i + 1]] for i in range(len(sizes))]

def rms_norm(x, w):
    xf = x.astype(jnp.float32)
    y = xf * lax.rsqrt(jnp.mean(xf * xf, axis=-1, keepdims=True) + EPS)
    return (y * w.astype(jnp.float32)).astype(x.dtype)

def l2_norm(x):
    return x * lax.rsqrt(jnp.sum(x * x, axis=-1, keepdims=True) + EPS)

def rope_tables(positions, dim):
    inv_freq = ROPE_THETA ** (-jnp.arange(0, dim, 2, dtype=jnp.float32) / dim)
    ang = positions.astype(jnp.float32)[..., None] * inv_freq
    return jnp.cos(ang), jnp.sin(ang)

def apply_rope(x, cos, sin):
    shape = cos.shape[:2] + (1,) * (x.ndim - 3) + cos.shape[2:]
    c, s = cos.reshape(shape), sin.reshape(shape)
    x1, x2 = jnp.split(x.astype(jnp.float32), 2, axis=-1)
    return jnp.concatenate([x1 * c - x2 * s, x2 * c + x1 * s], axis=-1)

def causal_conv(x, w):
    K = w.shape[0]
    T = x.shape[1]
    xp = jnp.pad(x, ((0, 0), (K - 1, 0), (0, 0)))
    return sum(xp[:, i:i + T] * w[i] for i in range(K))

def causal_mask(start, T):
    return (start + jnp.arange(Q_BLOCK))[:, None] >= jnp.arange(T)[None, :]

def block_starts(T):
    return jnp.arange(T // Q_BLOCK) * Q_BLOCK

def gated_delta_rule(q, k, v, g, beta):
    B, H, T, dk = q.shape
    dv = v.shape[-1]
    C = GDN_CHUNK
    N = T // C
    chunk = lambda t: t.reshape(B, H, N, C, *t.shape[3:])
    q = chunk(q * dk ** -0.5)
    k = chunk(k)
    v = chunk(v)
    beta = chunk(beta)
    gc = jnp.cumsum(chunk(g), axis=-1)
    incl = jnp.tril(jnp.ones((C, C), dtype=bool))
    strict = jnp.tril(jnp.ones((C, C), dtype=bool), -1)
    decay = jnp.where(incl, jnp.exp(jnp.where(incl, gc[..., :, None] - gc[..., None, :], 0.0)), 0.0)
    kb = k * beta[..., None]
    kk = jnp.einsum('bhncd,bhnsd->bhncs', kb, k) * decay
    a_mat = jnp.where(strict, kk, 0.0) + jnp.eye(C, dtype=kk.dtype)
    rhs = jnp.concatenate([v * beta[..., None], kb * jnp.exp(gc)[..., None]], axis=-1)
    sol = lax.linalg.triangular_solve(a_mat, rhs, left_side=True, lower=True, unit_diagonal=True)
    u, w = sol[..., :dv], sol[..., dv:]
    qk = jnp.where(incl, jnp.einsum('bhncd,bhnsd->bhncs', q, k) * decay, 0.0)
    q_dec = q * jnp.exp(gc)[..., None]
    k_dec = k * jnp.exp(gc[..., -1:] - gc)[..., None]
    g_last = jnp.exp(gc[..., -1])

    def step(S, xs):
        qd, kd, uc, wc, qkc, gl = xs
        v_new = uc - jnp.einsum('bhcd,bhde->bhce', wc, S)
        o = jnp.einsum('bhcd,bhde->bhce', qd, S) + jnp.einsum('bhcs,bhse->bhce', qkc, v_new)
        S = S * gl[..., None, None] + jnp.einsum('bhcd,bhce->bhde', kd, v_new)
        return S, o

    xs = tuple(jnp.moveaxis(t, 2, 0) for t in (q_dec, k_dec, u, w, qk, g_last))
    S0 = jnp.zeros((B, H, dk, dv), jnp.float32)
    _, o = lax.scan(step, S0, xs)
    return jnp.moveaxis(o, 0, 2).reshape(B, H, T, dv)

def diff_attention(q, k, v, lam):
    B, T, H, _, d = q.shape
    dv = v.shape[-1]
    qh = q.transpose(0, 2, 3, 1, 4).astype(jnp.float32) * d ** -0.5
    kh = k.transpose(0, 2, 3, 1, 4).astype(jnp.float32)
    vh = v.transpose(0, 2, 1, 3).astype(jnp.float32)

    def block(start):
        qb = lax.dynamic_slice_in_dim(qh, start, Q_BLOCK, axis=3)
        s = jnp.einsum('bhmqd,bhmkd->bhmqk', qb, kh)
        a = jax.nn.softmax(jnp.where(causal_mask(start, T), s, NEG_INF), axis=-1)
        a = a[:, :, 0] - lam * a[:, :, 1]
        return jnp.einsum('bhqk,bhkd->bhqd', a, vh)

    o = lax.map(block, block_starts(T))
    return o.transpose(1, 0, 3, 2, 4).reshape(B, T, H, dv)

def even_mixer(h, cos, sin, w_in, conv_w, a_log, dt_bias, gdn_norm_w,
               lam_q1, lam_k1, lam_q2, lam_k2, diff_norm_w, w_out, lambda_init):
    B, T, _ = h.shape
    qkv_a, z_a, b_a, a_a, q_b, k_b, v_b = split_cols(h @ w_in, EVEN_SPLITS)
    qkv_a = jax.nn.silu(causal_conv(qkv_a, conv_w))
    q_a, k_a, v_a = split_cols(qkv_a, [GDN_QK, GDN_QK, GDN_V])
    to_heads = lambda t: t.reshape(B, T, GDN_HEADS, GDN_HEAD_DIM).transpose(0, 2, 1, 3).astype(jnp.float32)
    q_a = l2_norm(to_heads(q_a))
    k_a = l2_norm(to_heads(k_a))
    v_a = to_heads(v_a)
    beta = jax.nn.sigmoid(b_a.astype(jnp.float32)).transpose(0, 2, 1)
    g = (-jnp.exp(a_log.astype(jnp.float32))
         * jax.nn.softplus(a_a.astype(jnp.float32) + dt_bias.astype(jnp.float32))).transpose(0, 2, 1)
    o_a = gated_delta_rule(q_a, k_a, v_a, g, beta).transpose(0, 2, 1, 3)
    z = z_a.reshape(B, T, GDN_HEADS, GDN_HEAD_DIM).astype(jnp.float32)
    o_a = rms_norm(o_a, gdn_norm_w) * jax.nn.silu(z)
    q_b = apply_rope(q_b.reshape(B, T, DIFF_HEADS, 2, DIFF_QK_DIM), cos, sin)
    k_b = apply_rope(k_b.reshape(B, T, DIFF_HEADS, 2, DIFF_QK_DIM), cos, sin)
    v_b = v_b.reshape(B, T, DIFF_HEADS, DIFF_V_DIM)
    lam = (jnp.exp(jnp.sum(lam_q1.astype(jnp.float32) * lam_k1.astype(jnp.float32)))
           - jnp.exp(jnp.sum(lam_q2.astype(jnp.float32) * lam_k2.astype(jnp.float32))) + lambda_init)
    o_b = diff_attention(q_b, k_b, v_b, lam)
    o_b = rms_norm(o_b, diff_norm_w) * (1.0 - lambda_init)
    o = jnp.concatenate([o_a.reshape(B, T, GDN_V), o_b.reshape(B, T, DIFF_V)], axis=-1)
    return o.astype(h.dtype) @ w_out

def fox_mixer(h, w_in, b_forget, w_out):
    B, T, _ = h.shape
    q, k, v, gate, f = split_cols(h @ w_in, ODD_SPLITS)
    heads = lambda t: t.reshape(B, T, FOX_HEADS, FOX_HEAD_DIM).transpose(0, 2, 1, 3).astype(jnp.float32)
    qh = heads(q) * FOX_HEAD_DIM ** -0.5
    kh = heads(k)
    vh = heads(v)
    log_f = jax.nn.log_sigmoid(f.astype(jnp.float32) + b_forget.astype(jnp.float32))
    cum = jnp.cumsum(log_f, axis=1).transpose(0, 2, 1)

    def block(start):
        qb = lax.dynamic_slice_in_dim(qh, start, Q_BLOCK, axis=2)
        cb = lax.dynamic_slice_in_dim(cum, start, Q_BLOCK, axis=2)
        s = jnp.einsum('bhqd,bhkd->bhqk', qb, kh) + cb[..., :, None] - cum[:, :, None, :]
        a = jax.nn.softmax(jnp.where(causal_mask(start, T), s, NEG_INF), axis=-1)
        return jnp.einsum('bhqk,bhkd->bhqd', a, vh)

    o = lax.map(block, block_starts(T))
    o = o.transpose(1, 0, 3, 2, 4).reshape(B, T, ODD_MIX)
    o = o * jax.nn.sigmoid(gate.astype(jnp.float32))
    return o.astype(h.dtype) @ w_out

def first_inputs(seed: int = 0) -> dict:
    key = jax.random.key(seed)
    ks = jax.random.split(key, 32)
    nrm = lambda k, shape, scale: jax.random.normal(k, shape, jnp.float32) * scale
    gain = lambda k, shape: 1.0 + 0.02 * jax.random.normal(k, shape, jnp.float32)
    dt = jnp.exp(jax.random.uniform(ks[7], (N_EVEN, GDN_HEADS), jnp.float32,
                                    math.log(0.001), math.log(0.1)))
    res_scale = (2.0 * DEPTH) ** -0.5
    return {
        'x': nrm(ks[0], (BATCH, SEQ, D_MODEL), 1.0),
        'p': nrm(ks[1], (DEPTH, BATCH, SEQ, PLE_DIM), 1.0),
        'positions': jnp.broadcast_to(jnp.arange(SEQ, dtype=jnp.int32), (BATCH, SEQ)),
        'norm_mix': gain(ks[2], (DEPTH, D_MODEL)),
        'norm_mlp': gain(ks[3], (DEPTH, D_MODEL)),
        'norm_final': gain(ks[4], (D_MODEL,)),
        'w_in_even': nrm(ks[5], (N_EVEN, D_MODEL, EVEN_IN), D_MODEL ** -0.5),
        'conv_w': nrm(ks[6], (N_EVEN, CONV_WIDTH, 3 * GDN_QK), CONV_WIDTH ** -0.5),
        'a_log': jnp.log(jax.random.uniform(ks[8], (N_EVEN, GDN_HEADS), jnp.float32, 1.0, 16.0)),
        'dt_bias': dt + jnp.log(-jnp.expm1(-dt)),
        'gdn_norm': gain(ks[9], (N_EVEN, GDN_HEAD_DIM)),
        'lam_q1': nrm(ks[10], (N_EVEN, DIFF_QK_DIM), 0.1),
        'lam_k1': nrm(ks[11], (N_EVEN, DIFF_QK_DIM), 0.1),
        'lam_q2': nrm(ks[12], (N_EVEN, DIFF_QK_DIM), 0.1),
        'lam_k2': nrm(ks[13], (N_EVEN, DIFF_QK_DIM), 0.1),
        'diff_norm': gain(ks[14], (N_EVEN, DIFF_V_DIM)),
        'w_out_even': nrm(ks[15], (N_EVEN, EVEN_MIX, D_MODEL), EVEN_MIX ** -0.5 * res_scale),
        'w_in_odd': nrm(ks[16], (N_ODD, D_MODEL, ODD_IN), D_MODEL ** -0.5),
        'b_forget': jax.random.uniform(ks[17], (N_ODD, FOX_HEADS), jnp.float32, 1.0, 4.0),
        'w_out_odd': nrm(ks[18], (N_ODD, ODD_MIX, D_MODEL), ODD_MIX ** -0.5 * res_scale),
        'w_mlp_up': nrm(ks[19], (DEPTH, D_MODEL, D_FF), D_MODEL ** -0.5),
        'w_mlp_down': nrm(ks[20], (DEPTH, D_FF, D_MODEL), D_FF ** -0.5 * res_scale),
        'w_ple_proj': nrm(ks[21], (DEPTH, PLE_DIM, D_MODEL), PLE_DIM ** -0.5 * res_scale),
        'w_ple_gate': nrm(ks[22], (DEPTH, D_MODEL, D_MODEL), D_MODEL ** -0.5),
    }

def first_block(x, p, positions, norm_mix, norm_mlp, norm_final, w_in_even, conv_w, a_log, dt_bias,
              gdn_norm, lam_q1, lam_k1, lam_q2, lam_k2, diff_norm, w_out_even, w_in_odd, b_forget,
              w_out_odd, w_mlp_up, w_mlp_down, w_ple_proj, w_ple_gate):
    cos, sin = rope_tables(positions, DIFF_QK_DIM)
    for i in range(DEPTH):
        j = i // 2
        h = rms_norm(x, norm_mix[i])
        if i % 2 == 0:
            lambda_init = 0.8 - 0.6 * math.exp(-0.3 * i)
            y = even_mixer(h, cos, sin, w_in_even[j], conv_w[j], a_log[j], dt_bias[j], gdn_norm[j],
                           lam_q1[j], lam_k1[j], lam_q2[j], lam_k2[j], diff_norm[j], w_out_even[j],
                           lambda_init)
        else:
            y = fox_mixer(h, w_in_odd[j], b_forget[j], w_out_odd[j])
        x = x + y
        h = rms_norm(x, norm_mlp[i])
        x = x + jnp.square(jax.nn.relu(h @ w_mlp_up[i])) @ w_mlp_down[i]
        x = x + (p[i] @ w_ple_proj[i]) * jax.nn.sigmoid(x @ w_ple_gate[i])
    return rms_norm(x, norm_final)


_first_inputs = first_inputs


def first_inputs(seed=0):
    import zlib

    import numpy as np

    out = dict(_first_inputs(seed))
    spreads = {}
    factors = {'norm_mix': 4.271,
     'norm_mlp': 3.871,
     'norm_final': 2.874,
     'gdn_norm': 8.0,
     'lam_q1': 8.0,
     'lam_q2': 2.836,
     'diff_norm': 8.0,
     'b_forget': 3.984}
    for name, (base, spread) in spreads.items():
        noise = np.random.default_rng([zlib.crc32(name.encode()), seed]).standard_normal(out[name].shape)
        drawn = base * np.exp(spread * noise) if base else spread * noise
        out[name] = __import__('jax').numpy.asarray(drawn.astype(out[name].dtype))
    for name, factor in factors.items():
        out[name] = (out[name] * factor).astype(out[name].dtype)
    return out


GRID_W = 64
CTX_LEN = 256
N_MIXERS = 2
EXPAND = 2
E_WIDTH = EXPAND * D_MODEL
HEAD_K = 128
N_HEADS = E_WIDTH // HEAD_K
HEAD_V = E_WIDTH // N_HEADS
CHUNK = 16
CONV_W = 31


def _rmsnorm(x, g):
    xf = x.astype(jnp.float32)
    y = xf * lax.rsqrt(jnp.mean(xf * xf, axis=-1, keepdims=True) + EPS)
    return (y * g.astype(jnp.float32)).astype(x.dtype)

def _layernorm(x, g, b):
    xf = x.astype(jnp.float32)
    xc = xf - jnp.mean(xf, axis=-1, keepdims=True)
    var = jnp.mean(xc * xc, axis=-1, keepdims=True)
    return (xc * lax.rsqrt(var + EPS) * g.astype(jnp.float32) + b.astype(jnp.float32)).astype(x.dtype)

def _ada(cvec, w, b):
    m = jax.nn.silu(cvec) @ w + b
    return jnp.split(m, 3, axis=-1)

def _modulate(x, g, shift, scale):
    return _rmsnorm(x, g) * (1 + scale) + shift

def _hgrn_lower_bounds(lb_logits):
    p = jax.nn.softmax(lb_logits.astype(jnp.float32), axis=1)
    return jnp.cumsum(p, axis=1) - p[:, :1]

def _heads(t):
    return t.reshape(t.shape[0], t.shape[1], N_HEADS, -1).astype(jnp.float32)

def _forget(z, lb):
    f = lb + (1 - lb) * jax.nn.sigmoid(z.astype(jnp.float32))
    return _heads(jnp.log(f)), _heads(1 - f)

def _chunk_gla(q, k, v, g, s0):
    b_, length, h_, _ = q.shape
    n = length // CHUNK

    def to_chunks(t):
        return t.reshape(b_, n, CHUNK, h_, t.shape[-1]).transpose(1, 0, 3, 2, 4)

    mask = jnp.tril(jnp.ones((CHUNK, CHUNK), dtype=bool))
    mid = CHUNK // 2

    def step(state, inp):
        qc, kc, vc, gc = inp
        bcum = jnp.cumsum(gc, axis=-2)
        b_ref = bcum[..., mid:mid + 1, :]
        b_end = bcum[..., -1:, :]
        inter = jnp.einsum('bhck,bhkv->bhcv', qc * jnp.exp(bcum), state)
        scores = jnp.einsum('bhtk,bhsk->bhts', qc * jnp.exp(bcum - b_ref), kc * jnp.exp(b_ref - bcum))
        intra = jnp.einsum('bhts,bhsv->bhtv', jnp.where(mask, scores, 0.0), vc)
        new_state = (jnp.exp(b_end[..., 0, :])[..., None] * state
                     + jnp.einsum('bhsk,bhsv->bhkv', kc * jnp.exp(b_end - bcum), vc))
        return new_state, inter + intra

    s_final, o = lax.scan(step, s0, (to_chunks(q), to_chunks(k), to_chunks(v), to_chunks(g)))
    o = o.transpose(1, 0, 3, 2, 4).reshape(b_, length, h_, v.shape[-1])
    return o, s_final

def _chunk_gla_rev(q, k, v, g, s0):
    flip = lambda t: jnp.flip(t, axis=1)
    o, s_final = _chunk_gla(flip(q), flip(k), flip(v), flip(g), s0)
    return flip(o), s_final

def _hgrn_project(h, w_in, lb_f, lb_b):
    p = h @ w_in
    q, v, zf, zb, gate = jnp.split(p, 5, axis=-1)
    gf, kf = _forget(zf, lb_f)
    gb, kb = _forget(zb, lb_b)
    return _heads(jax.nn.silu(q)), _heads(v), gf, kf, gb, kb, gate

def _hgrn_readout(o, gate, norm_g, w_out):
    o = _rmsnorm(o, norm_g)
    o = o.reshape(o.shape[0], o.shape[1], E_WIDTH).astype(gate.dtype)
    return (o * jax.nn.silu(gate)) @ w_out

def _hgrn2_mixer(h, hc, w_in, lb_f, lb_b, norm_g, w_out, need_ctx):
    q, v, gf, kf, gb, kb, gate = _hgrn_project(h, w_in, lb_f, lb_b)
    qc, vc, gfc, kfc, gbc, kbc, gatec = _hgrn_project(hc, w_in, lb_f, lb_b)
    s0 = jnp.zeros((hc.shape[0], N_HEADS, HEAD_K, HEAD_V), jnp.float32)
    oc_f, sc_f = _chunk_gla(qc, kfc, vc, gfc, s0)
    oc_b, sc_b = _chunk_gla_rev(qc, kbc, vc, gbc, s0)
    o_f, _ = _chunk_gla(q, kf, v, gf, sc_f)
    o_b, _ = _chunk_gla_rev(q, kb, v, gb, sc_b)
    y = _hgrn_readout(o_f + o_b, gate, norm_g, w_out)
    yc = _hgrn_readout(oc_f + oc_b, gatec, norm_g, w_out) if need_ctx else None
    return y, yc

def _dwconv(u, w, b):
    pad = CONV_W // 2
    out = lax.conv_general_dilated(u, w[:, None, :], window_strides=(1,), padding=[(pad, pad)],
                                   dimension_numbers=('NWC', 'WIO', 'NWC'),
                                   feature_group_count=u.shape[-1])
    return out + b

def _latent_dwconv(u, w, b, vertical):
    b_, length, ch = u.shape
    rows = length // GRID_W
    grid = u.reshape(b_, rows, GRID_W, ch)
    if vertical:
        grid = grid.transpose(0, 2, 1, 3)
    n1, n2 = grid.shape[1], grid.shape[2]
    out = _dwconv(grid.reshape(b_ * n1, n2, ch), w, b).reshape(b_, n1, n2, ch)
    if vertical:
        out = out.transpose(0, 2, 1, 3)
    return out.reshape(b_, length, ch)

def _conv_mixer(h, w_in, b_in, dw, dw_b, ln_g, ln_b, w_out, b_out, conv_fn):
    p = h @ w_in + b_in
    a, gl, gate = jnp.split(p, 3, axis=-1)
    u = a * jax.nn.sigmoid(gl)
    u = conv_fn(u, dw, dw_b)
    u = jax.nn.silu(_layernorm(u, ln_g, ln_b))
    return (u * jax.nn.silu(gate)) @ w_out + b_out

def second_inputs(seed: int = 0) -> dict:
    key = jax.random.key(seed)
    ks = jax.random.split(key, 20)
    n_a = (DEPTH + 1) // 2
    n_b = DEPTH // 2
    f32 = jnp.float32

    def w(k, shape, fan_in):
        return jax.random.normal(k, shape, f32) * fan_in ** -0.5

    def small(k, shape, s=0.02):
        return jax.random.normal(k, shape, f32) * s

    return {
        "x": jax.random.normal(ks[0], (BATCH, SEQ, D_MODEL), f32),
        "c": jax.random.normal(ks[1], (BATCH, D_MODEL), f32),
        "ctx": jax.random.normal(ks[2], (BATCH, CTX_LEN, D_MODEL), f32),
        "c_ctx": jax.random.normal(ks[3], (D_MODEL,), f32),
        "norm_g": 1.0 + small(ks[4], (DEPTH, D_MODEL)),
        "ada_w": w(ks[5], (DEPTH, D_MODEL, 3 * D_MODEL), D_MODEL),
        "ada_b": small(ks[6], (DEPTH, 3 * D_MODEL)),
        "hgrn_w_in": w(ks[7], (n_a, D_MODEL, 5 * E_WIDTH), D_MODEL),
        "hgrn_lb_logits": small(ks[8], (2, n_a, E_WIDTH), 0.1),
        "hgrn_norm_g": 1.0 + small(ks[9], (n_a, HEAD_V)),
        "hgrn_w_out": w(ks[10], (n_a, E_WIDTH, D_MODEL), E_WIDTH),
        "conv_w_in": w(ks[11], (n_b, D_MODEL, 3 * E_WIDTH), D_MODEL),
        "conv_b_in": small(ks[12], (n_b, 3 * E_WIDTH)),
        "conv_dw": w(ks[13], (n_b, CONV_W, E_WIDTH), CONV_W),
        "conv_dw_b": small(ks[14], (n_b, E_WIDTH)),
        "conv_ln_g": 1.0 + small(ks[15], (n_b, E_WIDTH)),
        "conv_ln_b": small(ks[16], (n_b, E_WIDTH)),
        "conv_w_out": w(ks[17], (n_b, E_WIDTH, D_MODEL), E_WIDTH),
        "conv_b_out": small(ks[18], (n_b, D_MODEL)),
        "final_norm_g": 1.0 + small(ks[19], (D_MODEL,)),
    }

def second_block(x, c, ctx, c_ctx, norm_g, ada_w, ada_b, hgrn_w_in, hgrn_lb_logits, hgrn_norm_g, hgrn_w_out,
              conv_w_in, conv_b_in, conv_dw, conv_dw_b, conv_ln_g, conv_ln_b, conv_w_out, conv_b_out,
              final_norm_g):
    lb = _hgrn_lower_bounds(hgrn_lb_logits)
    for i in range(DEPTH):
        mixer = i % N_MIXERS
        j = i // N_MIXERS
        need_ctx = any(m % N_MIXERS == 0 for m in range(i + 1, DEPTH))
        shift, scale, gate = _ada(c, ada_w[i], ada_b[i])
        h = _modulate(x, norm_g[i], shift[:, None], scale[:, None])
        if mixer == 0 or need_ctx:
            shift_c, scale_c, gate_c = _ada(c_ctx, ada_w[i], ada_b[i])
            hc = _modulate(ctx, norm_g[i], shift_c, scale_c)
        if mixer == 0:
            y, yc = _hgrn2_mixer(h, hc, hgrn_w_in[j], lb[0, j], lb[1, j], hgrn_norm_g[j], hgrn_w_out[j], need_ctx)
        else:
            vertical = (j % 2 == 1)
            lat_conv = lambda u, dw, dwb: _latent_dwconv(u, dw, dwb, vertical)
            y = _conv_mixer(h, conv_w_in[j], conv_b_in[j], conv_dw[j], conv_dw_b[j], conv_ln_g[j], conv_ln_b[j],
                            conv_w_out[j], conv_b_out[j], lat_conv)
            yc = (_conv_mixer(hc, conv_w_in[j], conv_b_in[j], conv_dw[j], conv_dw_b[j], conv_ln_g[j], conv_ln_b[j],
                              conv_w_out[j], conv_b_out[j], _dwconv) if need_ctx else None)
        x = x + gate[:, None] * y
        if need_ctx:
            ctx = ctx + gate_c * yc
    return _rmsnorm(x, final_norm_g)


_first_inputs_2 = second_inputs


def second_inputs(seed=0):
    import zlib

    import numpy as np

    out = dict(_first_inputs_2(seed))
    spreads = {}
    factors = {}
    for name, (base, spread) in spreads.items():
        noise = np.random.default_rng([zlib.crc32(name.encode()), seed]).standard_normal(out[name].shape)
        drawn = base * np.exp(spread * noise) if base else spread * noise
        out[name] = __import__('jax').numpy.asarray(drawn.astype(out[name].dtype))
    for name, factor in factors.items():
        out[name] = (out[name] * factor).astype(out[name].dtype)
    return out


_narrow_inputs = second_inputs


def second_inputs(seed=0):

    out = dict(_narrow_inputs(seed))
    wider = {'ctx': 8.81,
     'c_ctx': 9.73,
     'norm_g': 5.02,
     'hgrn_norm_g': 6.29,
     'conv_b_in': 10.69,
     'conv_dw_b': 8.26,
     'conv_ln_g': 9.41,
     'conv_ln_b': 11.87,
     'conv_b_out': 6.23,
     'final_norm_g': 3.16}
    for name, times in wider.items():
        mean = out[name].mean()
        out[name] = (mean + times * (out[name] - mean)).astype(out[name].dtype)
    return out


N_EVEN_3 = (DEPTH + 1) // 2
N_ODD_3 = DEPTH // 2
RMS_EPS = 1e-6
A_WIDTH = D_MODEL
CONV_WIDTH_3 = 3
B_WIDTH = D_MODEL
B_GROUPS = 8
CHUNK_3 = 128
SGU_LN_EPS = 1e-5
C_WIDTH = D_MODEL
C_HEAD_DIM = 64
C_HEADS = C_WIDTH // C_HEAD_DIM
DECAY_LORA = 64
AAA_LORA = 64
GN_EPS = 64e-5
RWKV_STREAM = 3 * C_WIDTH + DECAY_LORA + AAA_LORA
RWKV_SPLITS = (C_WIDTH, 2 * C_WIDTH, 3 * C_WIDTH, 3 * C_WIDTH + DECAY_LORA)
D_WIDTH = D_MODEL // 2
D_GROUPS = 4
D_GROUP_DIM = D_WIDTH // D_GROUPS
EVEN_PROJ = 4 * A_WIDTH + 3 * B_WIDTH
EVEN_SPLITS_3 = (A_WIDTH, 2 * A_WIDTH, 3 * A_WIDTH, 4 * A_WIDTH,
               4 * A_WIDTH + B_WIDTH, 4 * A_WIDTH + 2 * B_WIDTH)
ODD_PROJ = RWKV_STREAM + C_WIDTH + 2 * D_WIDTH
ODD_SPLITS_3 = (RWKV_STREAM, RWKV_STREAM + C_WIDTH, RWKV_STREAM + C_WIDTH + D_WIDTH)


def rms_norm_3(x, g):
    xf = x.astype(jnp.float32)
    y = xf * lax.rsqrt(jnp.mean(xf * xf, axis=-1, keepdims=True) + RMS_EPS)
    return (y * g.astype(jnp.float32)).astype(x.dtype)

def layer_norm(x, g, b, eps):
    xf = x.astype(jnp.float32)
    mu = jnp.mean(xf, axis=-1, keepdims=True)
    var = jnp.mean(jnp.square(xf - mu), axis=-1, keepdims=True)
    y = (xf - mu) * lax.rsqrt(var + eps)
    return (y * g + b).astype(x.dtype)

def shift_prev(p):
    pad = [(0, 0)] * (p.ndim - 2) + [(1, 0), (0, 0)]
    return jnp.pad(p, pad)[..., :-1, :]

def shift_next(p):
    pad = [(0, 0)] * (p.ndim - 2) + [(0, 1), (0, 0)]
    return jnp.pad(p, pad)[..., 1:, :]

def short_conv_branch(h, gate_b, gate_c, conv_w):
    xc = gate_c * h
    y = conv_w[0] * shift_prev(xc) + conv_w[1] * xc + conv_w[2] * shift_next(xc)
    return gate_b * y

def chunked_sgu_branch(u, v, ln_g, ln_b, w_s, b_s):
    bsz, s, c = v.shape
    vn = layer_norm(v, ln_g, ln_b, SGU_LN_EPS)
    vc = vn.reshape(bsz, s // CHUNK_3, CHUNK_3, B_GROUPS, c // B_GROUPS)
    mixed = jnp.einsum('gij,bnjgd->bnigd', w_s, vc) + b_s.T[:, :, None]
    return u * mixed.reshape(bsz, s, c)

def wkv7_step(state, inp):
    r, w, k, v, a, b = inp
    sa = jnp.einsum('...ij,...j->...i', state, a)
    state = (state * w[..., None, :] + sa[..., :, None] * b[..., None, :]
             + v[..., :, None] * k[..., None, :])
    y = jnp.einsum('...ij,...j->...i', state, r)
    return state, y

def rwkv7_bidir_branch(p, mu, w0, w2, a0, a2, k_k, k_a, r_k, lnx_g, lnx_b):
    dtype = p.dtype
    bsz, s, _ = p.shape
    pf = p.astype(jnp.float32)
    shifted = jnp.stack([shift_prev(pf), shift_next(pf)])
    q = pf[None] + mu[:, None, None, :] * (shifted - pf[None])
    r, k, v, wd, ad = jnp.split(q, RWKV_SPLITS, axis=-1)
    z_w = w0[:, None, None, :] + jnp.einsum('dbsl,dlc->dbsc', jnp.tanh(wd), w2)
    decay = jnp.exp(-jnp.exp(-jax.nn.softplus(-z_w) - 0.5))
    a = jax.nn.sigmoid(a0[:, None, None, :] + jnp.einsum('dbsl,dlc->dbsc', ad, a2))
    heads = lambda t: t.reshape(t.shape[:3] + (C_HEADS, C_HEAD_DIM))
    kk = heads(k * k_k)
    kk = kk * lax.rsqrt(jnp.maximum(jnp.sum(kk * kk, axis=-1, keepdims=True), 1e-12))
    k = k * (1.0 + (a - 1.0) * k_a)
    r, k, v, decay, a = heads(r), heads(k), heads(v), heads(decay), heads(a)

    def to_scan(t):
        t = jnp.stack([t[0], jnp.flip(t[1], axis=1)])
        return jnp.moveaxis(t, 2, 0)

    init = jnp.zeros((2, bsz, C_HEADS, C_HEAD_DIM, C_HEAD_DIM), jnp.float32)
    xs = (to_scan(r), to_scan(decay), to_scan(k), to_scan(v), to_scan(-kk), to_scan(kk * a))
    _, y = lax.scan(wkv7_step, init, xs)
    y = jnp.moveaxis(y, 0, 2)
    y_sum = y[0] + jnp.flip(y[1], axis=1)
    out = layer_norm(y_sum, lnx_g.reshape(C_HEADS, C_HEAD_DIM),
                     lnx_b.reshape(C_HEADS, C_HEAD_DIM), GN_EPS)
    bonus = jnp.sum(r * k * r_k, axis=-1, keepdims=True) * v
    out = out + bonus[0] + bonus[1]
    return out.reshape(bsz, s, C_WIDTH).astype(dtype)

def fourier_branch(f, w_f):
    bsz, s, c = f.shape
    fg = f.reshape(bsz, s, D_GROUPS, D_GROUP_DIM).astype(jnp.float32)
    spec = jnp.fft.fft2(fg, axes=(1, 3), norm="ortho").real.astype(f.dtype)
    y = jnp.einsum('bsgd,gde->bsge', spec, w_f)
    return y.reshape(bsz, s, c)

def even_layer(h, w_in, conv_w, sgu_ln_g, sgu_ln_b, sgu_w, sgu_b, w_out):
    p = jnp.einsum('bsd,de->bse', h, w_in)
    xa, ba, ca, za, ub, vb, zb = jnp.split(p, EVEN_SPLITS_3, axis=-1)
    ya = short_conv_branch(xa, ba, ca, conv_w) * jax.nn.silu(za)
    yb = chunked_sgu_branch(ub, vb, sgu_ln_g, sgu_ln_b, sgu_w, sgu_b) * jax.nn.silu(zb)
    return jnp.einsum('bse,ed->bsd', jnp.concatenate([ya, yb], axis=-1), w_out)

def odd_layer(h, w_in, mu, w0, w2, a0, a2, k_k, k_a, r_k, lnx_g, lnx_b, fnet_w, w_out):
    p = jnp.einsum('bsd,de->bse', h, w_in)
    pc, zc, fd, zd = jnp.split(p, ODD_SPLITS_3, axis=-1)
    yc = rwkv7_bidir_branch(pc, mu, w0, w2, a0, a2, k_k, k_a, r_k, lnx_g, lnx_b) * jax.nn.silu(zc)
    yd = fourier_branch(fd, fnet_w) * jax.nn.silu(zd)
    return jnp.einsum('bse,ed->bsd', jnp.concatenate([yc, yd], axis=-1), w_out)

def third_inputs(seed: int = 0) -> dict:
    key = jax.random.key(seed)
    ks = iter(jax.random.split(key, 32))
    nrm = lambda shape, scale: scale * jax.random.normal(next(ks), shape, jnp.float32)
    NE, NO = N_EVEN_3, N_ODD_3
    return {
        "x": nrm((BATCH, SEQ, D_MODEL), 1.0),
        "e_norm_g": 1.0 + nrm((NE, D_MODEL), 0.02),
        "e_w_in": nrm((NE, D_MODEL, EVEN_PROJ), D_MODEL ** -0.5),
        "e_conv_w": nrm((NE, CONV_WIDTH_3, A_WIDTH), CONV_WIDTH_3 ** -0.5),
        "e_sgu_ln_g": 1.0 + nrm((NE, B_WIDTH), 0.02),
        "e_sgu_ln_b": nrm((NE, B_WIDTH), 0.02),
        "e_sgu_w": nrm((NE, B_GROUPS, CHUNK_3, CHUNK_3), CHUNK_3 ** -0.5),
        "e_sgu_b": 1.0 + nrm((NE, B_GROUPS, CHUNK_3), 0.01),
        "e_w_out": nrm((NE, A_WIDTH + B_WIDTH, D_MODEL), (A_WIDTH + B_WIDTH) ** -0.5),
        "o_norm_g": 1.0 + nrm((NO, D_MODEL), 0.02),
        "o_w_in": nrm((NO, D_MODEL, ODD_PROJ), D_MODEL ** -0.5),
        "o_mu": jax.random.uniform(next(ks), (NO, 2, RWKV_STREAM), jnp.float32),
        "o_w0": nrm((NO, 2, C_WIDTH), 0.5),
        "o_w2": nrm((NO, 2, DECAY_LORA, C_WIDTH), 0.5 * DECAY_LORA ** -0.5),
        "o_a0": nrm((NO, 2, C_WIDTH), 0.1),
        "o_a2": nrm((NO, 2, AAA_LORA, C_WIDTH), 0.5 * AAA_LORA ** -0.5),
        "o_k_k": 0.85 + nrm((NO, C_WIDTH), 0.05),
        "o_k_a": 1.0 + nrm((NO, C_WIDTH), 0.05),
        "o_r_k": nrm((NO, C_HEADS, C_HEAD_DIM), 0.1),
        "o_lnx_g": 1.0 + nrm((NO, C_WIDTH), 0.02),
        "o_lnx_b": nrm((NO, C_WIDTH), 0.02),
        "o_fnet_w": nrm((NO, D_GROUPS, D_GROUP_DIM, D_GROUP_DIM), D_GROUP_DIM ** -0.5),
        "o_w_out": nrm((NO, C_WIDTH + D_WIDTH, D_MODEL), (C_WIDTH + D_WIDTH) ** -0.5),
        "final_norm_g": 1.0 + nrm((D_MODEL,), 0.02),
    }

def third_block(x, e_norm_g, e_w_in, e_conv_w, e_sgu_ln_g, e_sgu_ln_b, e_sgu_w, e_sgu_b, e_w_out,
              o_norm_g, o_w_in, o_mu, o_w0, o_w2, o_a0, o_a2, o_k_k, o_k_a, o_r_k,
              o_lnx_g, o_lnx_b, o_fnet_w, o_w_out, final_norm_g):
    h = x
    for layer in range(DEPTH):
        i = layer // 2
        if layer % 2 == 0:
            h = h + even_layer(rms_norm_3(h, e_norm_g[i]), e_w_in[i], e_conv_w[i],
                               e_sgu_ln_g[i], e_sgu_ln_b[i], e_sgu_w[i], e_sgu_b[i], e_w_out[i])
        else:
            h = h + odd_layer(rms_norm_3(h, o_norm_g[i]), o_w_in[i], o_mu[i], o_w0[i], o_w2[i],
                              o_a0[i], o_a2[i], o_k_k[i], o_k_a[i], o_r_k[i],
                              o_lnx_g[i], o_lnx_b[i], o_fnet_w[i], o_w_out[i])
    return rms_norm_3(h, final_norm_g)


_first_inputs_3 = third_inputs


def third_inputs(seed=0):
    import zlib

    import numpy as np

    out = dict(_first_inputs_3(seed))
    spreads = {}
    factors = {'e_sgu_ln_g': 6.849,
     'e_sgu_ln_b': 6.314,
     'e_sgu_b': 8.0,
     'o_norm_g': 3.369,
     'o_a0': 2.876,
     'o_k_k': 8.0,
     'o_k_a': 2.685,
     'o_lnx_g': 7.893,
     'o_lnx_b': 8.0,
     'final_norm_g': 2.909}
    for name, (base, spread) in spreads.items():
        noise = np.random.default_rng([zlib.crc32(name.encode()), seed]).standard_normal(out[name].shape)
        drawn = base * np.exp(spread * noise) if base else spread * noise
        out[name] = __import__('jax').numpy.asarray(drawn.astype(out[name].dtype))
    for name, factor in factors.items():
        out[name] = (out[name] * factor).astype(out[name].dtype)
    return out


_narrow_inputs_3 = third_inputs


def third_inputs(seed=0):

    out = dict(_narrow_inputs_3(seed))
    wider = {'e_sgu_b': 4.02, 'o_k_k': 12.0, 'o_lnx_g': 7.73, 'o_lnx_b': 7.91, 'final_norm_g': 3.27}
    for name, times in wider.items():
        mean = out[name].mean()
        out[name] = (mean + times * (out[name] - mean)).astype(out[name].dtype)
    return out


def setup_inputs(seed=0):
    out = dict(first_inputs(seed))
    for name, value in second_inputs(seed + 1).items():
        if name != "x":
            out[name + "_2"] = value
    for name, value in third_inputs(seed + 2).items():
        if name != "x":
            out[name + "_3"] = value
    return out


def reference(
    x, p, positions, norm_mix, norm_mlp, norm_final, w_in_even, conv_w, a_log, dt_bias,
    gdn_norm, lam_q1, lam_k1, lam_q2, lam_k2, diff_norm, w_out_even, w_in_odd, b_forget,
    w_out_odd, w_mlp_up, w_mlp_down, w_ple_proj, w_ple_gate, c_2, ctx_2, c_ctx_2, norm_g_2,
    ada_w_2, ada_b_2, hgrn_w_in_2, hgrn_lb_logits_2, hgrn_norm_g_2, hgrn_w_out_2, conv_w_in_2,
    conv_b_in_2, conv_dw_2, conv_dw_b_2, conv_ln_g_2, conv_ln_b_2, conv_w_out_2, conv_b_out_2,
    final_norm_g_2, e_norm_g_3, e_w_in_3, e_conv_w_3, e_sgu_ln_g_3, e_sgu_ln_b_3, e_sgu_w_3,
    e_sgu_b_3, e_w_out_3, o_norm_g_3, o_w_in_3, o_mu_3, o_w0_3, o_w2_3, o_a0_3, o_a2_3, o_k_k_3,
    o_k_a_3, o_r_k_3, o_lnx_g_3, o_lnx_b_3, o_fnet_w_3, o_w_out_3, final_norm_g_3,
):
    x = first_block(
        x, p, positions, norm_mix, norm_mlp, norm_final, w_in_even, conv_w, a_log, dt_bias,
        gdn_norm, lam_q1, lam_k1, lam_q2, lam_k2, diff_norm, w_out_even, w_in_odd, b_forget,
        w_out_odd, w_mlp_up, w_mlp_down, w_ple_proj, w_ple_gate,
    )
    x = second_block(
        x, c_2, ctx_2, c_ctx_2, norm_g_2, ada_w_2, ada_b_2, hgrn_w_in_2, hgrn_lb_logits_2,
        hgrn_norm_g_2, hgrn_w_out_2, conv_w_in_2, conv_b_in_2, conv_dw_2, conv_dw_b_2,
        conv_ln_g_2, conv_ln_b_2, conv_w_out_2, conv_b_out_2, final_norm_g_2,
    )
    return third_block(
        x, e_norm_g_3, e_w_in_3, e_conv_w_3, e_sgu_ln_g_3, e_sgu_ln_b_3, e_sgu_w_3, e_sgu_b_3,
        e_w_out_3, o_norm_g_3, o_w_in_3, o_mu_3, o_w0_3, o_w2_3, o_a0_3, o_a2_3, o_k_k_3,
        o_k_a_3, o_r_k_3, o_lnx_g_3, o_lnx_b_3, o_fnet_w_3, o_w_out_3, final_norm_g_3,
    )


_drawn_inputs = setup_inputs


def setup_inputs(seed=0):
    import zlib

    import numpy as np

    out = dict(_drawn_inputs(seed))
    spreads = {}
    factors = {}
    for name, (base, spread) in spreads.items():
        noise = np.random.default_rng([zlib.crc32(name.encode()), seed]).standard_normal(out[name].shape)
        drawn = base * np.exp(spread * noise) if base else spread * noise
        out[name] = __import__('jax').numpy.asarray(drawn.astype(out[name].dtype))
    for name, factor in factors.items():
        out[name] = (out[name] * factor).astype(out[name].dtype)
    return out
```

```python
from contextlib import ExitStack

import numpy as np
import concourse.bass as bass
from concourse import mybir
from concourse.alu_op_type import AluOpType as ALU

F32 = mybir.dt.float32
I32 = mybir.dt.int32
ACT = mybir.ActivationFunctionType
AX = mybir.AxisListType.X
ds = bass.ds

P = 128
T = 512
TT = T // P
D = 1024
KD = D // P
FF = 4 * D
CTX = 256
HG = 16
EPS = 1e-6
NEG = -1e30
TILE = 8 * 512
CREDIT = 64


def const_tables():
    i = np.arange(P)
    a, b = i[:, None], i[None, :]
    same = (a // 64) == (b // 64)
    c = {}
    c["ident"] = (a == b)
    c["ones"] = np.ones((P, P))
    c["same64"] = same
    c["le64"] = same & (a <= b)
    c["ge64"] = same & (a >= b)
    c["lt64"], c["gt64"] = same & (a < b), same & (a > b)
    for n, z in enumerate((1, 2, 4, 8, 16, 32, 64)):
        pair = (a // (2 * z)) == (b // (2 * z))
        c[f"low{n}"] = pair & ((a // z) % 2 == 1) & ((b // z) % 2 == 0)
    for n, z in enumerate((1, 2, 4, 8, 16, 32, 64)):
        pair = (a // (2 * z)) == (b // (2 * z))
        c[f"up{n}"] = pair & ((a // z) % 2 == 0) & ((b // z) % 2 == 1)
    c["causal"] = np.where(b > a, NEG, 0.0)
    block16 = (a // 16) == (b // 16)
    c["diag_f"] = block16 & (a <= b)
    c["diag_b"] = block16 & (a >= b)
    t = np.arange(T)[None, :]
    c["resets_f"] = np.broadcast_to(t % P != 0, (P, T))
    c["resets_b"] = np.broadcast_to(t % P != P - 1, (P, T))
    half = (a // 32) % 2
    c["rot"] = np.where((half == 1) & (b == a - 32), -1.0, 0.0) + np.where((half == 0) & (b == a + 32), 1.0, 0.0)
    inv = np.float32(10000.0) ** (-np.arange(0, 64, 2, dtype=np.float32) / np.float32(64))
    c["invfreq"] = inv[i % 32][:, None]
    c["eps"] = np.full((P, 1), EPS)
    c["eps5"] = np.full((P, 1), 1e-5)
    c["eps_gn"] = np.full((P, 1), 64e-5)
    c["scale64"], c["scale128"] = np.full((P, 1), 64 ** -0.5), np.full((P, 1), 128 ** -0.5)
    c["one"] = np.full((P, 1), 1.0)
    return c


CONST = {}
_at = 0
for _n, _v in const_tables().items():
    CONST[_n] = (_at, _v.shape[1])
    _at += _v.shape[1]
NCONST = _at


class Sig:

    def __init__(self, sem):
        self.sem, self.n = sem, CREDIT


class Core:

    def __init__(self, nc, ctx):
        self.nc, self.ctx, self.sigs = nc, ctx, {}
        self.tile = 0

    def sb(self, name, shape, dt=F32):
        return self.ctx.enter_context(self.nc.sbuf_tensor(name, shape, dt))

    def declare(self, name):
        self.sigs[name] = Sig(self.ctx.enter_context(self.nc.semaphore(name)))
        return self.sigs[name].sem

    def count(self, name, n):
        return self.sigs[name].n + n

    def apart(self, eng):
        eng.sem_inc(self.carried, 1)

    def sem(self, name):
        return self.sigs[name].sem

    def done(self, **counts):
        for name, n in counts.items():
            self.sigs[name].n += n

    def c(self, name):
        at, n = CONST[name]
        return self.const[:, at:at + n]

    def v(self, name):
        at, n = VEC[name]
        return self.vecs[:, at:at + n]

    def big(self, at, n):
        assert at + n <= NBIG, (at, n, NBIG)
        return self.bigbuf[:, at:at + n]


VECS = [("norm_mix0", 8), ("norm_mix1", 8), ("norm_mlp0", 8), ("norm_mlp1", 8), ("norm_final", 8),
        ("w_forget", 64), ("b_forget", 1), ("w_ba", 64),
        ("conv_w", 48), ("a_log", 4), ("dt_bias", 16), ("gdn_norm", 1), ("diff_norm", 1), ("lams", 256),
        ("c_vecs", 16), ("ada_b0", 24), ("ada_b1", 24), ("norm_g0", 8), ("norm_g1", 8), ("hgrn_norm", 1), ("norm_final2", 8),
        ("conv_b_in", 48), ("conv_dw", 496), ("conv_dw_b", 16), ("conv_ln_g", 16), ("conv_ln_b", 16), ("conv_b_out", 8),
        ("e_norm", 8), ("short_w", 24), ("norm_final3", 8), ("o_norm", 8), ("mu0", 25), ("mu1", 25), ("w0_0", 8), ("w0_1", 8), ("a0_0", 8), ("a0_1", 8),
        ("k_k", 8), ("k_a", 8), ("r_k", 8), ("lnx_g", 8), ("lnx_b", 8)]
VEC, NVEC = {}, 0
for _n, _w in VECS:
    VEC[_n] = (NVEC, _w)
    NVEC += _w
NBIG = 56 * T


def col(v):
    return np.asarray(v).reshape(-1, P).T


def rows(v):
    v = np.asarray(v).reshape(-1)
    return np.concatenate([v, np.zeros(P - v.size, v.dtype)])[:, None]


def glu_order(w):
    r = w[:, 0:4096].reshape(-1, 2, 8, 256)
    return r.transpose(0, 2, 1, 3).reshape(-1, 4096)


def host_vecs(a):
    d = {}
    for i in range(2):
        d[f"norm_mix{i}"] = col(a["norm_mix"][i])
        d[f"norm_mlp{i}"] = col(a["norm_mlp"][i])
    d["norm_final"] = col(a["norm_final"])
    d["w_forget"] = a["w_in_odd"][0][:, 4096:].reshape(8, P, 8).transpose(1, 0, 2).reshape(P, 64)
    d["b_forget"] = rows(a["b_forget"][0])
    d["w_ba"] = a["w_in_even"][0][:, 2048:2056].reshape(8, P, 8).transpose(1, 0, 2).reshape(P, 64)
    d["conv_w"] = a["conv_w"][0].reshape(4, 12, P).transpose(2, 1, 0).reshape(P, 48)
    every = lambda v: np.broadcast_to(np.asarray(v).reshape(1, -1), (P, np.asarray(v).size))
    d["a_log"] = every(a["a_log"][0])
    d["dt_bias"] = every(np.tile(a["dt_bias"][0], TT))
    d["gdn_norm"], d["diff_norm"] = col(a["gdn_norm"][0]), col(a["diff_norm"][0])
    d["lams"] = every(np.concatenate([a[n][0] for n in ("lam_q1", "lam_k1", "lam_q2", "lam_k2")]))
    d["c_vecs"] = np.stack([col(a["c_2"][0]), col(a["c_ctx_2"])], axis=2).reshape(P, 16)
    for i in range(2):
        d[f"ada_b{i}"] = col(a["ada_b_2"][i])
        d[f"norm_g{i}"] = col(a["norm_g_2"][i])
    d["hgrn_norm"] = col(a["hgrn_norm_g_2"][0])
    d["norm_final2"] = col(a["final_norm_g_2"])
    d["conv_b_in"] = np.concatenate([glu_order(a["conv_b_in_2"][0][None])[0], a["conv_b_in_2"][0][4096:]])
    d["conv_b_in"] = col(d["conv_b_in"])
    d["conv_dw"] = a["conv_dw_2"][0].reshape(31, 16, P).transpose(2, 1, 0).reshape(P, 496)
    d["conv_dw_b"], d["conv_ln_g"], d["conv_ln_b"] = (col(a[n][0]) for n in ("conv_dw_b_2", "conv_ln_g_2", "conv_ln_b_2"))
    d["conv_b_out"] = col(a["conv_b_out_2"][0])
    d["e_norm"] = col(a["e_norm_g_3"][0])
    d["short_w"] = a["e_conv_w_3"][0].reshape(3, 8, P).transpose(2, 1, 0).reshape(P, 24)
    d["norm_final3"] = col(a["final_norm_g_3"])
    for i in range(2):
        d[f"mu{i}"] = col(a["o_mu_3"][0, i])
        d[f"w0_{i}"], d[f"a0_{i}"] = col(a["o_w0_3"][0, i]), col(a["o_a0_3"][0, i])
    d["o_norm"] = col(a["o_norm_g_3"][0])
    for n in ("k_k", "k_a", "r_k", "lnx_g", "lnx_b"):
        d[n] = col(a[f"o_{n}_3"][0])
    return np.concatenate([d[n] for n, _ in VECS], axis=1)


def tile_of(w):
    k = w.shape[0] // P
    t = w.reshape(k, P, 512).transpose(1, 0, 2).reshape(P, k * 512)
    return t if k == 8 else np.concatenate([t, np.zeros((P, TILE - k * 512), t.dtype)], axis=1)


def across(w, lo=0, hi=None):
    hi = w.shape[1] if hi is None else hi
    return [tile_of(w[:, n:n + 512]) for n in range(lo, hi, 512)]


def deep(w, rows_per=1024):
    return [tile_of(w[k:k + rows_per, n:n + 512]) for n in range(0, w.shape[1], 512) for k in range(0, w.shape[0], rows_per)]


def tiles_mlp(a, i):
    return across(a["w_mlp_up"][i]) + deep(a["w_mlp_down"][i])


def tiles_ple(a, i):
    w = a["w_ple_proj"][i]
    halves = [w[:, n:n + 512].reshape(2, P, 512).transpose(1, 0, 2).reshape(P, 1024) for n in (0, 512)]
    return [np.concatenate(halves + [np.zeros((P, 2048), w.dtype)], axis=1)] + across(a["w_ple_gate"][i])


def tiles_even(a):
    w = a["w_in_even"][0]
    return across(w, 0, 1536) + across(w, 2056, 3080) + across(w, 1536, 2048) + across(w, 3080, 3592) + \
        across(a["w_out_even"][0])


def tiles_hgrn(a):
    w = a["hgrn_w_in_2"][0].reshape(1024, 5, HG, P)
    heads = [tile_of(np.concatenate([w[:, n, h] for n in (0, 4, 2, 3)], axis=1)) for h in range(HG)]
    return across(a["ada_w_2"][0]) + heads + deep(a["hgrn_w_out_2"][0])


def values_hgrn(a):
    w = a["hgrn_w_in_2"][0].reshape(8, P, 5, HG, P)
    return np.ascontiguousarray(w[:, :, 1].transpose(2, 1, 0, 3).reshape(HG, P, 1024))


def tiles_conv(a):
    w = a["conv_w_in_2"][0]
    return across(a["ada_w_2"][1]) + across(glu_order(w)) + across(w, 4096) + deep(a["conv_w_out_2"][0])


def tiles_sgu(a):
    w = a["e_w_in_3"][0]
    cols = [0, 2, 1, 3, 4, 6, 5]
    return sum([across(w, 1024 * n, 1024 * (n + 1)) for n in cols], []) + deep(a["e_w_out_3"][0])


def tiles_rwkv(a):
    w = a["o_w_in_3"][0]
    short = np.concatenate([w[:, 3072:3200], np.zeros((D, 384), w.dtype)], axis=1)
    features = [tile_of(np.concatenate([w[:, n + c * P:n + (c + 1) * P] for n in (0, 1024, 2048, 3200)], axis=1))
                for c in range(KD)]
    return across(w, 4736, 5248) + across(w, 4224, 4736) + [tile_of(short)] + features + deep(a["o_w_out_3"][0], 768)


def dft_tables():
    t, d = np.arange(T), np.arange(P)
    at = 2 * np.pi * np.outer(t, t) / T
    af = 2 * np.pi * np.outer(d, d) / P
    over_t = np.concatenate([np.cos(at), np.sin(at)], axis=1) / np.sqrt(T)
    over_d = np.concatenate([np.cos(af), -np.sin(af)], axis=1) / np.sqrt(P)
    return over_t.reshape(TT, P, 2 * T).transpose(1, 0, 2).astype(np.float32), over_d.astype(np.float32)


def tiles_fox(a):
    return across(a["w_in_odd"][0], 0, 4096) + across(a["w_out_odd"][0])


def fori(eng, n, body):
    if n == 1:
        body(0)
    else:
        with eng.Fori(0, n) as i:
            body(i)


def wait_tile(K, eng, r, off, slot):
    eng.wait_ge(K.landed[slot], 16 * ((K.tile + off) // 2 + 1) + 16 * r)


def tiles(K, eng, count, body):
    pairs = count // 2
    if pairs > 1:
        with eng.Fori(0, pairs) as r:
            for off in range(2):
                body(2 * r + off, r, off, (K.tile + off) % 2)
    elif pairs:
        for off in range(2):
            body(off, 0, off, (K.tile + off) % 2)
    if count % 2:
        body(count - 1, 0, count - 1, (K.tile + count - 1) % 2)


def prefetch(K, sp, count, used):
    def one(g, r, off, slot):
        used(g)
        sp.dma_start(K.W[:, slot, :], K.wstream[ds(K.tile + 2 + g, 1), :, :].rearrange("g p n -> p (g n)"))\
          .then_inc(K.landed[slot], 16)
    n = min(count, K.ntiles - 2 - K.tile)
    if n > 0:
        tiles(K, sp, n, one)


def linear(K, count, src, evac, sides=("act", "dve", "act", "dve"), nk=8, banks=4, token_major=False, width=T,
           follow=None):
    nc = K.nc
    per = {s: sum(x == s for x in sides[:banks]) for s in ("act", "dve")}
    with nc.Block() as block:
        @block.sync
        def _(sp):
            prefetch(K, sp, count, lambda g: sp.wait_ge(K.sem("product"), K.count("product", banks * (g + 1))))

        @block.tensor
        def _(pe):
            def one(g, r, off, slot):
                wait_tile(K, pe, r, off, slot)
                for s in ("act", "dve"):
                    if per[s]:
                        pe.wait_ge(K.sem(f"taken_{s}"), K.count(f"taken_{s}", per[s] * g - per[s]))
                w = K.W[:, slot, :].rearrange("p (k n) -> p k n", k=8)
                for j in range(banks):
                    for k in range(nk):
                        if token_major:
                            ops = (src[:, k, j * P:(j + 1) * P], w[:, k, :])
                        else:
                            ops = (w[:, k, j * P:(j + 1) * P], src[:, k, 0:width])
                        mm = pe.matmul(K.ps[:, 4 * slot + j, 0:T if token_major else width], *ops,
                                       start=(k == 0), stop=(k == nk - 1))
                    mm.then_inc(K.sem("product"), 1)
            tiles(K, pe, count, one)

        def takes(eng, side):
            def one(g, r, off, slot):
                for j in range(banks):
                    if sides[j] == side:
                        eng.wait_ge(K.sem("product"), K.count("product", banks * g + j + 1))
                        evac(eng, side, g, j, K.ps[:, 4 * slot + j, 0:T if token_major else width])\
                            .then_inc(K.sem(f"taken_{side}"), 1)
            if per[side]:
                tiles(K, eng, count, one)

        @block.scalar
        def _(act):
            takes(act, "act")

        @block.vector
        def _(dve):
            takes(dve, "dve")
            if follow is not None:
                def one(g, r, off, slot):
                    for j in range(banks):
                        dve.wait_ge(K.sem("taken_act"), K.count("taken_act", banks * g + j + 1))
                        follow(dve, g, j)
                tiles(K, dve, count, one)
    K.done(product=banks * count, followed=banks * count if follow else 0, taken_act=per["act"] * count, taken_dve=per["dve"] * count)
    K.tile += count


def linear_deep(K, kg_count, src, nks, add):
    nc = K.nc
    n = 2 * kg_count
    assert K.tile % 2 == 0 or kg_count % 2 == 0

    with nc.Block() as block:
        @block.sync
        def _(sp):
            def body(m):
                for kg in range(kg_count):
                    if kg < kg_count - 1:
                        sp.wait_ge(K.sem("tile_used"), K.count("tile_used", (kg_count - 1) * m + kg + 1))
                    else:
                        sp.wait_ge(K.sem("product"), K.count("product", 4 * (m + 1)))
                    slot = (K.tile + kg) % 2
                    if K.tile + 2 + n <= K.ntiles or not isinstance(m, int):
                        sp.dma_start(K.W[:, slot, :], K.wstream[ds(K.tile + 2 + m * kg_count + kg, 1), :, :]
                                     .rearrange("g p n -> p (g n)")).then_inc(K.landed[slot], 16)
            if K.tile + 2 + n <= K.ntiles:
                fori(sp, 2, body)
            else:
                for m in range(2):
                    for kg in range(kg_count):
                        if K.tile + 2 + m * kg_count + kg >= K.ntiles:
                            return
                        if kg < kg_count - 1:
                            sp.wait_ge(K.sem("tile_used"), K.count("tile_used", (kg_count - 1) * m + kg + 1))
                        else:
                            sp.wait_ge(K.sem("product"), K.count("product", 4 * (m + 1)))
                        t = K.tile + 2 + m * kg_count + kg
                        sp.dma_start(K.W[:, t % 2, :], K.wstream[t, :, :]).then_inc(K.landed[t % 2], 16)

        @block.tensor
        def _(pe):
            with pe.Fori(0, 2) as m:
                for kg in range(kg_count):
                    slot = (K.tile + kg) % 2
                    pe.wait_ge(K.landed[slot], 16 * ((K.tile + kg) // 2 + 1) + m * (16 * kg_count // 2))
                    w = K.W[:, slot, :].rearrange("p (k n) -> p k n", k=8)
                    for j in range(4):
                        for k in range(nks):
                            mm = pe.matmul(K.psflat[:, ds(m * 2048 + j * 512, 512)], w[:, k, j * P:(j + 1) * P],
                                           src(kg * nks + k), start=(kg == 0 and k == 0),
                                           stop=(kg == kg_count - 1 and k == nks - 1), skip_group_check=True)
                        if kg == kg_count - 1:
                            mm.then_inc(K.sem("product"), 1)
                    if kg < kg_count - 1:
                        mm.then_inc(K.sem("tile_used"), 1)

        @block.vector
        def _(dve):
            with dve.Fori(0, 2) as m:
                for j in range(4):
                    dve.wait_ge(K.sem("product"), K.count("product", 4 * m + j + 1))
                    add(dve, m, j, K.psflat[:, ds(m * 2048 + j * 512, 512)])
    K.done(product=8, tile_used=2 * (kg_count - 1))
    K.tile += n


def tiles_in(flat):
    return lambda k: flat[:, k * T:(k + 1) * T]


def add_to(x):
    flat = x.rearrange("p k t -> p (k t)")

    def add(dve, m, j, ps):
        at = flat[:, ds(m * 2048 + j * 512, 512)]
        dve.tensor_tensor(at, ps, at, ALU.add)
    return add


def norm(K, src, dst, gain, width=T, shift=None):
    nc = K.nc
    sq, ln, rstd, ps = K.sq, K.ln, K.rstd, K.ps[:, 0, 0:width]
    with nc.Block() as block:
        @block.tensor
        def _(pe):
            for k in range(KD):
                pe.wait_ge(K.sem("square"), K.count("square", k + 1))
                pe.matmul(ps, K.c("ones"), sq[:, k % 2, 0:width], start=(k == 0), stop=(k == KD - 1))\
                  .then_inc(K.sem("summed"), 1)

        @block.scalar
        def _(act):
            for k in range(KD):
                act.wait_ge(K.sem("summed"), K.count("summed", k - 1))
                act.activation(sq[:, k % 2, 0:width], src[:, k, 0:width], ACT.Square).then_inc(K.sem("square"), 1)
            act.wait_ge(K.sem("summed"), K.count("summed", KD))
            act.activation(ln[:, 0:width], ps, ACT.Ln, scale=1.0 / D, bias=K.c("eps")).then_inc(K.sem("logged"), 1)
            act.wait_ge(K.sem("logged"), K.count("logged", 1))
            act.activation(rstd[:, 0:width], ln[:, 0:width], ACT.Exp, scale=-0.5).then_inc(K.sem("rstd"), 1)

        @block.vector
        def _(dve):
            dve.wait_ge(K.sem("rstd"), K.count("rstd", 1))
            for k in range(KD):
                dve.scalar_tensor_tensor(dst[:, k, 0:width], src[:, k, 0:width], gain[:, k:k + 1],
                                         rstd[:, 0:width], ALU.mult, ALU.mult).then_inc(K.sem("scaled"), 1)
            if shift is not None:
                for k in range(KD):
                    dve.wait_ge(K.sem("scaled"), K.count("scaled", k + 1))
                    dve.tensor_scalar(dst[:, k, 0:width], dst[:, k, 0:width], shift[:, k:k + 1], None, ALU.add)
    K.done(square=KD, summed=KD, logged=1, rstd=1, scaled=KD)


def mlp(K, layer):
    hid = K.big(0, 32 * T)

    def relu(eng, side, g, j, ps):
        return eng.activation(hid[:, ds(g * 2048 + j * 512, 512)], ps, ACT.Relu)

    def square(dve, g, j):
        at = hid[:, ds(g * 2048 + j * 512, 512)]
        dve.tensor_tensor(at, at, at, ALU.mult).then_inc(K.sem("followed"), 1)
    linear(K, 8, K.H, relu, sides=("act",) * 4, follow=square)
    linear_deep(K, 4, tiles_in(hid), 8, add_to(K.X))


def ple(K, layer):
    nc = K.nc
    pT = K.big(0, 2 * T).rearrange("p (k t) -> p k t", t=T)
    proj = K.big(2 * T, 8 * T)
    sig = K.big(10 * T, 8 * T)
    x, new = K.X.rearrange("p k t -> p (k t)"), K.H.rearrange("p k t -> p (k t)")
    first = K.tile
    with nc.Block() as block:
        @block.sync
        def _(sp):
            sp.dma_start(pT, K.ins["pT"][layer]).then_inc(K.sem("loaded"), 16)
            prefetch(K, sp, 1, lambda g: sp.wait_ge(K.sem("product"), K.count("product", 8)))

        @block.tensor
        def _(pe):
            wait_tile(K, pe, 0, 0, first % 2)
            pe.wait_ge(K.sem("loaded"), K.count("loaded", 16))
            w = K.W[:, first % 2, :].rearrange("p (k n) -> p k n", k=8)
            for n in range(8):
                for k in range(2):
                    mm = pe.matmul(K.ps[:, n, :], w[:, 2 * (n // 4) + k, (n % 4) * P:(n % 4 + 1) * P], pT[:, k, :],
                                   start=(k == 0), stop=(k == 1))
                mm.then_inc(K.sem("product"), 1)

        @block.vector
        def _(dve):
            for n in range(8):
                dve.wait_ge(K.sem("product"), K.count("product", n + 1))
                dve.tensor_copy(proj[:, n * T:(n + 1) * T], K.ps[:, n, :])
    K.done(product=8, loaded=16)
    K.tile += 1

    def sigmoid(eng, side, g, j, ps):
        return eng.activation(sig[:, ds(g * 2048 + j * 512, 512)], ps, ACT.Sigmoid)

    def gated(dve, g, j):
        s = ds(g * 2048 + j * 512, 512)
        dve.tensor_tensor(sig[:, s], sig[:, s], proj[:, s], ALU.mult).then_inc(K.sem("gated"), 1)
        dve.wait_ge(K.sem("gated"), K.count("gated", 4 * g + j + 1))
        dve.tensor_tensor(new[:, s], x[:, s], sig[:, s], ALU.add).then_inc(K.sem("followed"), 1)
    linear(K, 2, K.X, sigmoid, sides=("act",) * 4, follow=gated)
    K.done(gated=8)
    K.X, K.H = K.H, K.X


def skew(eng, n, head, tail):
    head(0, 0)
    with eng.Fori(0, n // 2 - 1) as r:
        head(2 * r + 1, 1)
        tail(2 * r, 0)
        head(2 * r + 2, 0)
        tail(2 * r + 1, 1)
    head(n - 1, 1)
    tail(n - 2, 0)
    tail(n - 1, 1)


def attention(K, heads, maps, q, k, v, scale, out, gate=None, cum=None, neg_lam=None, base=0):
    nc = K.nc
    dk = P // maps
    at = base

    def room(n):
        nonlocal at
        at += n
        return K.big(at - n, n)
    qs, ks, vs = (room(2 * T).rearrange("p (b t) -> p b t", b=2) for _ in range(3))
    probs = room(2 * maps * TT * T).rearrange("p (b m i t) -> p b m i t", b=2, m=maps, i=TT)
    turned = room(TT * T).rearrange("p (i t) -> p i t", i=TT)
    peak = K.small[:, 0:0 + 2 * maps * TT].rearrange("p (b m i) -> p b m i", b=2, m=maps)
    total = K.small[:, 16:16 + 2 * maps * TT].rearrange("p (b m i) -> p b m i", b=2, m=maps)
    inv = K.small[:, 32:32 + 2 * maps * TT].rearrange("p (b m i) -> p b m i", b=2, m=maps)
    N = maps * TT
    flat = lambda t: t.rearrange("p h t -> p (h t)")
    vf = v.rearrange("p i n -> p (i n)")

    with nc.Block() as block:
        @block.gpsimd
        def _(pool):
            def one(h, b):
                pool.wait_ge(K.sem("mixed"), K.count("mixed", h - 1))
                pool.tensor_tensor(qs[:, b, :], flat(q)[:, ds(h * T, T)], K.c(scale).broadcast_to([P, T]), ALU.mult)\
                    .then_inc(K.sem("q_fixed"), 1)
                pool.tensor_copy(ks[:, b, :], flat(k)[:, ds(h * T, T)]).then_inc(K.sem("k_fixed"), 1)
                pool.tensor_copy(vs[:, b, :].rearrange("p (i n) -> p i n", i=TT),
                                 v[:, :, ds(h * P, P)]).then_inc(K.sem("v_fixed"), 1)
            with pool.Fori(0, heads // 2) as r:
                one(2 * r, 0)
                one(2 * r + 1, 1)

        @block.tensor
        def _(pe):
            def scores(h, b):
                pe.wait_ge(K.sem("q_fixed"), K.count("q_fixed", h + 1))
                pe.wait_ge(K.sem("k_fixed"), K.count("k_fixed", h + 1))
                for i in range(TT):
                    w = (i + 1) * P
                    for m in range(maps):
                        n = i * maps + m
                        ps = K.ps[:, n % 4, :]
                        pe.wait_ge(K.sem("probs"), K.count("probs", N * h + n - 3))
                        rows = slice(m * dk, (m + 1) * dk)
                        pe.matmul(ps[:, 0:w], qs[rows, b, i * P:w], ks[rows, b, 0:w], start=True, stop=False,
                                  skip_group_check=True)
                        if cum is not None:
                            pe.matmul(ps[:, 0:w], K.c("ones")[0:heads, :], cum[0:heads, ds(h * T, w)],
                                      start=False, stop=False, skip_group_check=True)
                        pe.matmul(ps[:, i * P:w], K.c("ident"), K.c("causal"), start=False, stop=True,
                                  skip_group_check=True).then_inc(K.sem("scores"), 1)

            def mix(h, b):
                pe.wait_ge(K.sem("v_fixed"), K.count("v_fixed", h + 1))
                for i in range(TT):
                    pe.wait_ge(K.sem("weights"), K.count("weights", TT * h + i + 1))
                    pe.wait_ge(K.sem("turned_kept"), K.count("turned_kept", TT * h + i - 1))
                    for s in range(i + 1):
                        t = pe.transpose(K.ps[:, 4 + i % 2, s * P:(s + 1) * P], probs[:, b, 0, i, s * P:(s + 1) * P],
                                         K.c("ident"))
                    t.then_inc(K.sem("turned"), 1)
                pe.wait_ge(K.sem("turned_kept"), K.count("turned_kept", TT * (h + 1)))
                pe.wait_ge(K.sem("head_out"), K.count("head_out", h - 1))
                for s in range(TT):
                    mm = pe.matmul(K.ps[:, 6 + b, s * P:T], vs[:, b, s * P:(s + 1) * P], turned[:, s, s * P:T],
                                   start=(s == 0), stop=(s == TT - 1), skip_group_check=True)
                mm.then_inc(K.sem("mixed"), 1)
            skew(pe, heads, scores, mix)

        @block.scalar
        def _(act):
            def exps(h, b):
                for i in range(TT):
                    w = (i + 1) * P
                    if i == 0:
                        act.wait_ge(K.sem("turned"), K.count("turned", TT * h - TT))
                    for m in range(maps):
                        n = i * maps + m
                        act.wait_ge(K.sem("peak"), K.count("peak", N * h + n + 1))
                        act.activation(probs[:, b, m, i, 0:w], K.ps[:, n % 4, 0:w], ACT.Exp,
                                       bias=peak[:, b, m, i:i + 1], accum_out=total[:, b, m, i:i + 1])\
                           .then_inc(K.sem("probs"), 1)

            def keep(h, b):
                for i in range(TT):
                    act.wait_ge(K.sem("turned"), K.count("turned", TT * h + i + 1))
                    act.wait_ge(K.sem("mixed"), K.count("mixed", h))
                    act.activation(turned[:, 0:i + 1, i * P:(i + 1) * P],
                                   K.ps[:, 4 + i % 2, 0:(i + 1) * P].rearrange("p (s t) -> p s t", t=P), ACT.Copy)\
                       .then_inc(K.sem("turned_kept"), 1)
            skew(act, heads, exps, keep)

        @block.vector
        def _(dve):
            def softmax(h, b):
                for i in range(TT):
                    w = (i + 1) * P
                    for m in range(maps):
                        n = i * maps + m
                        dve.wait_ge(K.sem("scores"), K.count("scores", N * h + n + 1))
                        dve.tensor_reduce(peak[:, b, m, i:i + 1], K.ps[:, n % 4, 0:w], AX, ALU.max, negate=True)\
                           .then_inc(K.sem("peak"), 1)
                for i in range(TT):
                    w = (i + 1) * P
                    dve.wait_ge(K.sem("probs"), K.count("probs", N * h + (i + 1) * maps))
                    dve.reciprocal(inv[:, b, :, i], total[:, b, :, i]).then_inc(K.sem("inverse"), 1)
                    dve.wait_ge(K.sem("inverse"), K.count("inverse", TT * h + i + 1))
                    p0 = probs[:, b, 0, i, 0:w]
                    if maps == 1:
                        dve.tensor_scalar(p0, p0, inv[:, b, 0, i:i + 1], None, ALU.mult)\
                           .then_inc(K.sem("weights"), 1)
                        continue
                    dve.tensor_scalar(p0, p0, inv[:, b, 0, i:i + 1], None, ALU.mult).then_inc(K.sem("first_map"), 1)
                    dve.tensor_scalar(probs[:, b, 1, i, 0:w], probs[:, b, 1, i, 0:w], inv[:, b, 1, i:i + 1],
                                      None, ALU.mult).then_inc(K.sem("second_map"), 1)
                    dve.wait_ge(K.sem("first_map"), K.count("first_map", TT * h + i + 1))
                    dve.wait_ge(K.sem("second_map"), K.count("second_map", TT * h + i + 1))
                    dve.scalar_tensor_tensor(p0, probs[:, b, 1, i, 0:w], neg_lam, p0, ALU.mult, ALU.add)\
                       .then_inc(K.sem("weights"), 1)

            def give(h, b):
                dve.wait_ge(K.sem("mixed"), K.count("mixed", h + 1))
                o = flat(out)[:, ds(h * T, T)]
                if gate is None:
                    dve.tensor_copy(o, K.ps[:, 6 + b, :]).then_inc(K.sem("head_out"), 1)
                else:
                    dve.tensor_tensor(o, K.ps[:, 6 + b, :], flat(gate)[:, ds(h * T, T)], ALU.mult)\
                       .then_inc(K.sem("head_out"), 1)
            skew(dve, heads, softmax, give)
    K.done(q_fixed=heads, k_fixed=heads, v_fixed=heads, scores=N * heads, peak=N * heads, probs=N * heads,
           inverse=TT * heads, weights=TT * heads, turned=TT * heads, turned_kept=TT * heads, mixed=heads,
           head_out=heads)
    if maps == 2:
        K.done(first_map=TT * heads, second_map=TT * heads)


def copy_to(dst, func=ACT.Copy):
    def evac(eng, side, g, j, ps):
        at = dst[:, ds(g * 2048 + j * 512, 512)]
        return eng.activation(at, ps, func) if side == "act" else eng.tensor_copy(at, ps)
    return evac


def plus_x(K):
    x = K.X.rearrange("p k t -> p (k t)")

    def evac(eng, side, g, j, ps):
        at = x[:, ds(g * 2048 + j * 512, 512)]
        return eng.tensor_tensor(at, ps, at, ALU.add)
    return evac


def tokens_to(dst, width):
    def evac(eng, side, g, j, ps):
        at = dst[:, ds(g * 512 + j * width, 512)]
        return eng.activation(at, ps, ACT.Copy) if side == "act" else eng.tensor_copy(at, ps)
    return evac


def fox(K):
    nc = K.nc
    q, k, v, gate = (K.big(n * 8 * T, 8 * T) for n in range(4))
    at = 4 * 8 * T
    cum = K.H.rearrange("p k t -> p (k t)")
    z = K.big(at, 6 * T).rearrange("p (n t) -> p n t", n=6)
    linear(K, 2, K.H, copy_to(q))
    linear(K, 2, K.H, copy_to(k))
    linear(K, 2, K.H, tokens_to(v, 1024), token_major=True)
    linear(K, 2, K.H, copy_to(gate, ACT.Sigmoid), sides=("act",) * 4)
    wf = K.v("w_forget").rearrange("p (k n) -> p k n", k=8)
    with nc.Block() as block:
        @block.tensor
        def _(pe):
            for n in range(8):
                mm = pe.matmul(K.ps[0:8, 0, :], wf[:, n, :], K.H[:, n, :], start=(n == 0), stop=(n == 7))
            mm.then_inc(K.sem("product"), 1)

        @block.vector
        def _(dve):
            dve.memset(z[0:8, 5, :], 1.0).then_inc(K.sem("step_dve"), 1)
            dve.wait_ge(K.sem("product"), K.count("product", 1))
            dve.tensor_scalar(z[0:8, 0, :], K.ps[0:8, 0, :], K.v("b_forget")[0:8, :], 0.0, ALU.add, ALU.min)\
               .then_inc(K.sem("step_dve"), 1)
            dve.wait_ge(K.sem("step_act"), K.count("step_act", 3))
            dve.wait_ge(K.sem("step_dve"), K.count("step_dve", 2))
            dve.tensor_tensor(z[0:8, 0, :], z[0:8, 0, :], z[0:8, 3, :], ALU.subtract).then_inc(K.sem("step_dve"), 1)
            dve.wait_ge(K.sem("step_dve"), K.count("step_dve", 3))
            dve.tensor_tensor_scan(z[0:8, 4, :], z[0:8, 5, :], z[0:8, 0, :], 0.0, ALU.mult, ALU.add)\
               .then_inc(K.sem("step_dve"), 1)
            dve.wait_ge(K.sem("step_dve"), K.count("step_dve", 4))
            for h in range(8):
                dve.tensor_scalar(cum[0:8, h * T:(h + 1) * T], z[0:8, 4, :], K.c("ident")[0:8, h:h + 1], -1.0,
                                  ALU.mult, ALU.mult)

        @block.scalar
        def _(act):
            act.wait_ge(K.sem("step_dve"), K.count("step_dve", 2))
            act.activation(z[0:8, 1, :], K.ps[0:8, 0, :], ACT.Abs, bias=K.v("b_forget")[0:8, :])\
               .then_inc(K.sem("step_act"), 1)
            act.wait_ge(K.sem("step_act"), K.count("step_act", 1))
            act.activation(z[0:8, 2, :], z[0:8, 1, :], ACT.Exp, scale=-1.0).then_inc(K.sem("step_act"), 1)
            act.wait_ge(K.sem("step_act"), K.count("step_act", 2))
            act.activation(z[0:8, 3, :], z[0:8, 2, :], ACT.Ln, bias=1.0).then_inc(K.sem("step_act"), 1)
    K.done(product=1, step_act=3, step_dve=4)
    h3 = lambda t: t.rearrange("p (h t) -> p h t", t=T)
    attention(K, 8, 1, h3(q), h3(k), v.rearrange("p (i n) -> p i n", n=1024), "scale128", h3(q), gate=h3(gate),
              cum=cum, base=at)
    linear(K, 2, h3(q), plus_x(K), sides=("dve",) * 4)


def head_norm(K, x, heads, gain, scale, gate=None, gain_step=0):
    nc = K.nc
    lnr = K.ln
    with nc.Block() as block:
        @block.scalar
        def _(act):
            def one(h, b):
                act.wait_ge(K.sem("summed"), K.count("summed", h - 1))
                act.activation(K.sq[:, b, :], x[:, ds(h * T, T)], ACT.Square).then_inc(K.sem("square"), 1)
                act.wait_ge(K.sem("summed"), K.count("summed", h + 1))
                act.activation(lnr[:, :], K.ps[:, b, :], ACT.Ln, scale=1.0 / P, bias=K.c("eps"))\
                   .then_inc(K.sem("logged"), 1)
                act.wait_ge(K.sem("logged"), K.count("logged", h + 1))
                act.wait_ge(K.sem("scaled"), K.count("scaled", h))
                act.activation(K.rstd[:, :], lnr[:, :], ACT.Exp, scale=-0.5).then_inc(K.sem("rstd"), 1)
            with act.Fori(0, heads // 2) as r:
                one(2 * r, 0)
                one(2 * r + 1, 1)

        @block.tensor
        def _(pe):
            def one(h, b):
                pe.wait_ge(K.sem("square"), K.count("square", h + 1))
                pe.matmul(K.ps[:, b, :], K.c("ones"), K.sq[:, b, :], start=True, stop=True)\
                  .then_inc(K.sem("summed"), 1)
            with pe.Fori(0, heads // 2) as r:
                one(2 * r, 0)
                one(2 * r + 1, 1)

        @block.vector
        def _(dve):
            dve.tensor_scalar(K.small[:, 100:101], gain, scale, None, ALU.mult).then_inc(K.sem("step_dve"), 1)
            dve.wait_ge(K.sem("step_dve"), K.count("step_dve", 1))
            with dve.Fori(0, heads) as h:
                dve.wait_ge(K.sem("rstd"), K.count("rstd", h + 1))
                at = x[:, ds(h * T, T)]
                dve.scalar_tensor_tensor(at, at, K.small[:, 100:101], K.rstd[:, :], ALU.mult, ALU.mult)\
                   .then_inc(K.sem("scaled"), 1)
                if gate is not None:
                    dve.wait_ge(K.sem("scaled"), K.count("scaled", h + 1))
                    dve.tensor_tensor(at, at, gate[:, ds(h * T, T)], ALU.mult)
    K.done(square=heads, summed=heads, logged=heads, rstd=heads, scaled=heads, step_dve=1)


def short_conv(K, x, y, n):
    nc = K.nc
    taps = K.v("conv_w")
    with nc.Block() as block:
        @block.vector
        def _(dve):
            with dve.Fori(0, n) as i:
                dve.tensor_scalar(y[:, ds(i * T, T)], x[:, ds(i * T, T)], taps[:, ds(i * 4 + 3, 1)], None, ALU.mult)\
                   .then_inc(K.sem("tap"), 1)
                for s in range(1, 4):
                    dve.wait_ge(K.sem("tap"), K.count("tap", 4 * i + s))
                    at = y[:, ds(i * T + s, T - s)]
                    dve.scalar_tensor_tensor(at, x[:, ds(i * T, T - s)], taps[:, ds(i * 4 + 3 - s, 1)], at,
                                             ALU.mult, ALU.add).then_inc(K.sem("tap"), 1)

        @block.scalar
        def _(act):
            with act.Fori(0, n) as i:
                act.wait_ge(K.sem("tap"), K.count("tap", 4 * i + 4))
                act.activation(y[:, ds(i * T, T)], y[:, ds(i * T, T)], ACT.Silu)
    K.done(tap=4 * n)


def gates(K, G, BETA, GC, BG, KDF):
    nc = K.nc
    w = K.v("w_ba").rearrange("p (k n) -> p k n", k=8)
    t = [K.small[:, 104 + 16 * n:120 + 16 * n] for n in range(7)]
    i4 = lambda a: a.rearrange("p (i h) -> p i h", i=TT)
    ps = K.ps[:, 0, 0:32].rearrange("p (i n) -> p i n", i=TT)
    with nc.Block() as block:
        @block.tensor
        def _(pe):
            for i in range(TT):
                for k in range(8):
                    mm = pe.matmul(K.ps[:, 0, 8 * i:8 * i + 8], K.H[:, k, i * P:(i + 1) * P], w[:, k, :],
                                   start=(k == 0), stop=(k == 7), skip_group_check=True)
            mm.then_inc(K.sem("step_pe"), 1)
            pe.wait_ge(K.sem("step_dve"), K.count("step_dve", 4))
            pe.matmul(K.ps[:, 1, 0:16], K.c("le64"), G, start=True, stop=True).then_inc(K.sem("step_pe"), 1)
            pe.matmul(K.ps[:, 2, 0:16], K.c("same64"), G, start=True, stop=True).then_inc(K.sem("step_pe"), 1)

        @block.scalar
        def _(act):
            act.wait_ge(K.sem("step_pe"), K.count("step_pe", 1))
            act.activation(i4(BETA), ps[:, :, 0:4], ACT.Sigmoid).then_inc(K.sem("step_act"), 1)
            act.activation(t[0][:, 0:4], K.v("a_log"), ACT.Exp).then_inc(K.sem("step_act"), 1)
            act.wait_ge(K.sem("step_dve"), K.count("step_dve", 1))
            act.activation(t[2], t[1], ACT.Abs).then_inc(K.sem("step_act"), 1)
            act.wait_ge(K.sem("step_act"), K.count("step_act", 3))
            act.activation(t[3], t[2], ACT.Exp, scale=-1.0).then_inc(K.sem("step_act"), 1)
            act.wait_ge(K.sem("step_act"), K.count("step_act", 4))
            act.activation(t[4], t[3], ACT.Ln, bias=1.0).then_inc(K.sem("step_act"), 1)
            act.wait_ge(K.sem("step_dve"), K.count("step_dve", 6))
            act.activation(t[5], GC, ACT.Exp).then_inc(K.sem("step_act"), 1)
            act.activation(KDF, t[6], ACT.Exp).then_inc(K.sem("step_act"), 1)

        @block.vector
        def _(dve):
            dve.wait_ge(K.sem("step_act"), K.count("step_act", 1))
            dve.tensor_tensor(i4(t[1]), ps[:, :, 4:8], K.v("dt_bias").rearrange("p (i h) -> p i h", i=TT), ALU.add)\
               .then_inc(K.sem("step_dve"), 1)
            dve.wait_ge(K.sem("step_act"), K.count("step_act", 5))
            dve.scalar_tensor_tensor(t[2], t[1], 0.0, t[4], ALU.max, ALU.add).then_inc(K.sem("step_dve"), 1)
            dve.wait_ge(K.sem("step_dve"), K.count("step_dve", 2))
            dve.tensor_scalar(t[3], t[2], -1.0, None, ALU.mult).then_inc(K.sem("step_dve"), 1)
            dve.wait_ge(K.sem("step_dve"), K.count("step_dve", 3))
            dve.tensor_tensor(i4(G), i4(t[3]), t[0][:, 0:4].unsqueeze(1).broadcast_to([P, TT, 4]), ALU.mult)\
               .then_inc(K.sem("step_dve"), 1)
            dve.wait_ge(K.sem("step_pe"), K.count("step_pe", 3))
            dve.tensor_copy(GC, K.ps[:, 1, 0:16]).then_inc(K.sem("step_dve"), 1)
            dve.wait_ge(K.sem("step_dve"), K.count("step_dve", 5))
            dve.tensor_tensor(t[6], K.ps[:, 2, 0:16], GC, ALU.subtract).then_inc(K.sem("step_dve"), 1)
            dve.wait_ge(K.sem("step_act"), K.count("step_act", 6))
            dve.tensor_tensor(BG, BETA, t[5], ALU.mult)
    K.done(step_pe=3, step_act=7, step_dve=6)


def invert(K, levels, X, XT, C, T1, A, masks, banks, n=4, tag=""):
    b0, b1, b2 = banks
    width = n * P

    def pool(pool, i):
        for l in range(levels):
            if l >= 2:
                pool.wait_ge(K.sem("half_turned"), K.count("half_turned", levels * i + l - 1))
            else:
                pool.wait_ge(K.sem("half_turned"), K.count("half_turned", levels * i))
            pool.tensor_tensor(C[:, l % 2], A, masks[l].unsqueeze(1).broadcast_to([P, n, P]), ALU.mult)\
                .then_inc(K.sem("between"), 1)

    def pe(pe, i):
        for l in range(levels):
            pe.wait_ge(K.sem("between"), K.count("between", levels * i + l + 1))
            pe.wait_ge(K.sem("inverse_kept"), K.count("inverse_kept", 2 * (levels * i + l) + i * 0))
            for h in range(n):
                mm = pe.matmul(K.ps[:, b0, h * P:(h + 1) * P], C[:, l % 2, h, :],
                               K.c("ident") if l == 0 else XT[:, h, :], start=True, stop=True)
            mm.then_inc(K.sem("half_turned"), 1)
            pe.wait_ge(K.sem("half_kept"), K.count("half_kept", levels * i + l + 1))
            for h in range(n):
                mm = pe.matmul(K.ps[:, b1, h * P:(h + 1) * P], T1[:, h, :],
                               K.c("ident") if l == 0 else X[:, h, :], start=True, stop=True)
            mm.then_inc(K.sem("correction"), 1)
            for h in range(n):
                mm = pe.matmul(K.ps[:, b2, h * P:(h + 1) * P], K.c("ident") if l == 0 else X[:, h, :],
                               T1[:, h, :], start=True, stop=True)
            mm.then_inc(K.sem("correction"), 1)

    def act(act, i):
        for l in range(levels):
            act.wait_ge(K.sem("half_turned"), K.count("half_turned", levels * i + l + 1))
            act.activation(T1, K.ps[:, b0, 0:width].rearrange("p (h t) -> p h t", t=P), ACT.Copy)\
               .then_inc(K.sem("half_kept"), 1)

    def dve(dve, i):
        for l in range(levels):
            ident = K.c("ident").unsqueeze(1).broadcast_to([P, n, P])
            for m, (b, x) in enumerate(((b1, X), (b2, XT))):
                dve.wait_ge(K.sem("correction"), K.count("correction", 2 * (levels * i + l) + 2))
                dve.wait_ge(K.sem("inverse_kept"), K.count("inverse_kept", 2 * (levels * i + l)))
                old = ident if l == 0 else x
                dve.tensor_tensor(x, old, K.ps[:, b, 0:width].rearrange("p (h t) -> p h t", t=P), ALU.subtract)\
                   .then_inc(K.sem("inverse_kept"), 1)
    return pool, pe, act, dve


def gated_delta(K, qkv, out, G, BETA, GC, BG, KDF, base):
    nc = K.nc
    NHD = 4
    free = [[0, 12 * T], [base, NBIG]]

    def room(n=NHD * P, m=1):
        region = next(r for r in free if r[0] + n * m <= r[1])
        region[0] += n * m
        r = K.big(region[0] - n * m, n * m)
        return r.rearrange("p (h t) -> p h t", t=P) if m == 1 else r.rearrange("p (m h t) -> p m h t", m=m, t=P)
    sq, rn = room(8 * P), room(8 * P)
    QN, KN, VF = room(), room(), room()
    KBG, KD_, VB = room(), room(), room()
    raw, dpos, E1, E2, EGR = room(), room(), room(), room(), room()
    A, QKT, X, XT, T1 = room(), room(), room(), room(), room()
    C = room(NHD * P, 2)
    WT, U, VN, S, QD = room(), room(), room(), room(), room()
    Gf = K.small[:, 80:84]
    x12 = qkv.rearrange("p (n t) -> p n t", t=T)
    o4 = out.rearrange("p (n t) -> p n t", t=T)
    bank = lambda b: K.ps[:, b, :].rearrange("p (h t) -> p h t", t=P)
    masks = [K.c(f"low{l}") for l in range(6)]
    per_head = lambda t, i: t[:, ds(4 * i, 4)].unsqueeze(2).broadcast_to([P, NHD, P])
    ipool, ipe, iact, idve = invert(K, 6, X, XT, C, T1, A, masks, (0, 1, 2))
    heads = range(NHD)

    with nc.Block() as block:
        @block.gpsimd
        def _(pool):
            pool.memset(S, 0.0).then_inc(K.sem("state"), 1)
            with pool.Fori(0, TT) as i:
                pool.wait_ge(K.sem("tokens_major"), K.count("tokens_major", 2 * i))
                pool.tensor_copy(VF, x12[:, 8:12, ds(i * P, P)]).then_inc(K.sem("v_fixed"), 1)
                pool.wait_ge(K.sem("a_ready"), K.count("a_ready", i + 1))
                ipool(pool, i)
                pool.wait_ge(K.sem("row_decay"), K.count("row_decay", i + 1))
                pool.wait_ge(K.sem("normed"), K.count("normed", 2 * (i + 1)))
                pool.wait_ge(K.sem("o_ready"), K.count("o_ready", 2 * i))
                pool.tensor_tensor(QD, QN, EGR, ALU.mult).then_inc(K.sem("q_decayed"), 1)

        @block.tensor
        def _(pe):
            with pe.Fori(0, TT) as i:
                pe.wait_ge(K.sem("square"), K.count("square", i + 1))
                for m in range(2):
                    mm = pe.matmul(K.ps[:, m, :], K.c("ones"), sq[:, 4 * m:4 * m + 4, :].rearrange("p h t -> p (h t)"),
                                   start=True, stop=True)
                mm.then_inc(K.sem("summed"), 1)
                pe.wait_ge(K.sem("normed"), K.count("normed", 2 * (i + 1)))
                pe.wait_ge(K.sem("v_fixed"), K.count("v_fixed", i + 1))
                for h in heads:
                    mm = pe.transpose(K.ps[:, 2, h * P:(h + 1) * P], KN[:, h, :], K.c("ident"))
                mm.then_inc(K.sem("tokens_major"), 1)
                for h in heads:
                    mm = pe.transpose(K.ps[:, 3, h * P:(h + 1) * P], VF[:, h, :], K.c("ident"))
                mm.then_inc(K.sem("tokens_major"), 1)
                pe.wait_ge(K.sem("g_fixed"), K.count("g_fixed", i + 1))
                pe.wait_ge(K.sem("o_ready"), K.count("o_ready", 2 * i))
                for h in heads:
                    mm = pe.matmul(K.ps[:, 6, h * P:(h + 1) * P], Gf[:, h:h + 1].broadcast_to([P, P]), K.c("le64"),
                                   start=True, stop=True)
                mm.then_inc(K.sem("row_sums"), 1)
                pe.wait_ge(K.sem("v_new"), K.count("v_new", 2 * i))
                for h in heads:
                    mm = pe.matmul(K.ps[:, 4, h * P:(h + 1) * P], KN[:, h, :], KN[:, h, :], start=True, stop=True)
                mm.then_inc(K.sem("scores"), 1)
                for h in heads:
                    mm = pe.matmul(K.ps[:, 5, h * P:(h + 1) * P], KN[:, h, :], QN[:, h, :], start=True, stop=True)
                mm.then_inc(K.sem("scores"), 1)
                pe.wait_ge(K.sem("scaled"), K.count("scaled", 3 * (i + 1)))
                ipe(pe, i)
                pe.wait_ge(K.sem("inverse_kept"), K.count("inverse_kept", 12 * (i + 1)))
                for h in heads:
                    mm = pe.matmul(K.ps[:, 3, h * P:(h + 1) * P], KBG[:, h, :], XT[:, h, :], start=True, stop=True)
                mm.then_inc(K.sem("solved"), 1)
                pe.wait_ge(K.sem("a_ready"), K.count("a_ready", i + 1))
                for h in heads:
                    mm = pe.matmul(K.ps[:, 4, h * P:(h + 1) * P], XT[:, h, :], VB[:, h, :], start=True, stop=True)
                mm.then_inc(K.sem("solved"), 1)
                pe.wait_ge(K.sem("solved_kept"), K.count("solved_kept", 2 * (i + 1)))
                pe.wait_ge(K.sem("q_decayed"), K.count("q_decayed", i + 1))
                pe.wait_ge(K.sem("qk_ready"), K.count("qk_ready", i + 1))
                for c in range(2):
                    n = 2 * i + c
                    r = slice(64 * c, 64 * c + 64)
                    pe.wait_ge(K.sem("state"), K.count("state", n + 1))
                    for h in heads:
                        mm = pe.matmul(K.ps[r, 5, h * P:(h + 1) * P], WT[:, h, r], S[:, h, :], start=True, stop=True,
                                       skip_group_check=True)
                    mm.then_inc(K.sem("recalled"), 1)
                    pe.wait_ge(K.sem("v_new"), K.count("v_new", n + 1))
                    pe.wait_ge(K.sem("o_ready"), K.count("o_ready", n))
                    for h in heads:
                        pe.matmul(K.ps[:, 6, h * 64:(h + 1) * 64], S[:, h, :], QD[:, h, r], start=True, stop=False,
                                  skip_group_check=True)
                        mm = pe.matmul(K.ps[:, 6, h * 64:(h + 1) * 64], VN[r, h, :], QKT[r, h, r], start=False,
                                       stop=True, skip_group_check=True)
                    mm.then_inc(K.sem("mixed"), 1)
                    for h in heads:
                        mm = pe.matmul(K.ps[:, 7, h * P:(h + 1) * P], KD_[r, h, :], VN[r, h, :], start=True, stop=True)
                    mm.then_inc(K.sem("learnt"), 1)

        @block.scalar
        def _(act):
            with act.Fori(0, TT) as i:
                act.activation(sq, x12[:, 0:8, ds(i * P, P)], ACT.Square).then_inc(K.sem("square"), 1)
                act.wait_ge(K.sem("summed"), K.count("summed", i + 1))
                ps2 = K.psflat[:, 0:1024]
                rn2, lg = rn.rearrange("p h t -> p (h t)"), sq.rearrange("p h t -> p (h t)")
                act.activation(lg, ps2, ACT.Ln, bias=K.c("eps")).then_inc(K.sem("logged"), 1)
                act.wait_ge(K.sem("logged"), K.count("logged", i + 1))
                act.wait_ge(K.sem("normed"), K.count("normed", 2 * i))
                act.activation(rn2, lg, ACT.Exp, scale=-0.5).then_inc(K.sem("rstd"), 1)
                act.wait_ge(K.sem("d_ready"), K.count("d_ready", 2 * i + 1))
                act.activation(EGR, bank(6), ACT.Exp).then_inc(K.sem("row_decay"), 1)
                act.wait_ge(K.sem("d_ready"), K.count("d_ready", 2 * i + 2))
                act.activation(E1, dpos, ACT.Exp, scale=-1.0).then_inc(K.sem("decay"), 1)
                act.activation(E2, raw, ACT.Exp).then_inc(K.sem("decay"), 1)
                iact(act, i)
                act.wait_ge(K.sem("solved"), K.count("solved", 2 * i + 1))
                act.activation(WT, bank(3), ACT.Copy).then_inc(K.sem("solved_kept"), 1)
                act.wait_ge(K.sem("solved"), K.count("solved", 2 * i + 2))
                act.activation(U, bank(4), ACT.Copy).then_inc(K.sem("solved_kept"), 1)
                for c in range(2):
                    act.wait_ge(K.sem("mixed"), K.count("mixed", 2 * i + c + 1))
                    act.activation(o4[:, 0:NHD, ds(i * P + 64 * c, 64)],
                                   K.ps[:, 6, 0:256].rearrange("p (h t) -> p h t", t=64), ACT.Copy)\
                       .then_inc(K.sem("o_ready"), 1)

        @block.vector
        def _(dve):
            with dve.Fori(0, TT) as i:
                dve.wait_ge(K.sem("row_sums"), K.count("row_sums", i))
                dve.tensor_copy(Gf, G[:, ds(4 * i, 4)]).then_inc(K.sem("g_fixed"), 1)
                dve.wait_ge(K.sem("rstd"), K.count("rstd", i + 1))
                dve.scalar_tensor_tensor(QN, x12[:, 0:4, ds(i * P, P)], P ** -0.5, rn[:, 0:4, :], ALU.mult, ALU.mult)\
                   .then_inc(K.sem("normed"), 1)
                dve.tensor_tensor(KN, x12[:, 4:8, ds(i * P, P)], rn[:, 4:8, :], ALU.mult).then_inc(K.sem("normed"), 1)
                dve.wait_ge(K.sem("tokens_major"), K.count("tokens_major", 2 * i + 1))
                dve.tensor_tensor(KBG, bank(2), per_head(BG, i), ALU.mult).then_inc(K.sem("scaled"), 1)
                dve.tensor_tensor(KD_, bank(2), per_head(KDF, i), ALU.mult).then_inc(K.sem("scaled"), 1)
                dve.wait_ge(K.sem("tokens_major"), K.count("tokens_major", 2 * i + 2))
                dve.tensor_tensor(VB, bank(3), per_head(BETA, i), ALU.mult).then_inc(K.sem("scaled"), 1)
                dve.wait_ge(K.sem("row_sums"), K.count("row_sums", i + 1))
                dve.tensor_tensor(raw, bank(6), per_head(GC, i), ALU.subtract).then_inc(K.sem("d_ready"), 1)
                dve.wait_ge(K.sem("d_ready"), K.count("d_ready", 2 * i + 1))
                dve.tensor_scalar(dpos, raw, 0.0, None, ALU.max).then_inc(K.sem("d_pos"), 1)
                dve.tensor_scalar(raw, raw, 0.0, None, ALU.min).then_inc(K.sem("d_ready"), 1)
                dve.wait_ge(K.sem("scores"), K.count("scores", 2 * i + 1))
                dve.tensor_tensor(A, bank(4), per_head(BETA, i), ALU.mult).then_inc(K.sem("a_beta"), 1)
                dve.wait_ge(K.sem("a_beta"), K.count("a_beta", i + 1))
                dve.wait_ge(K.sem("decay"), K.count("decay", 2 * i + 1))
                dve.tensor_tensor(A, A, E1, ALU.mult).then_inc(K.sem("a_ready"), 1)
                dve.wait_ge(K.sem("decay"), K.count("decay", 2 * i + 2))
                dve.tensor_tensor(E2, E2, K.c("le64").unsqueeze(1).broadcast_to([P, NHD, P]), ALU.mult)\
                   .then_inc(K.sem("masked"), 1)
                dve.wait_ge(K.sem("masked"), K.count("masked", i + 1))
                dve.wait_ge(K.sem("scores"), K.count("scores", 2 * i + 2))
                dve.tensor_tensor(QKT, bank(5), E2, ALU.mult).then_inc(K.sem("qk_ready"), 1)
                idve(dve, i)
                for c in range(2):
                    n = 2 * i + c
                    r = slice(64 * c, 64 * c + 64)
                    dve.wait_ge(K.sem("recalled"), K.count("recalled", n + 1))
                    dve.wait_ge(K.sem("solved_kept"), K.count("solved_kept", 2 * (i + 1)))
                    dve.tensor_tensor(VN[r], U[r], bank(5)[r], ALU.subtract).then_inc(K.sem("v_new"), 1)
                    dve.wait_ge(K.sem("row_decay"), K.count("row_decay", i + 1))
                    dve.wait_ge(K.sem("learnt"), K.count("learnt", n + 1))
                    last = EGR[:, :, 64 * c + 63:64 * c + 64].broadcast_to([P, NHD, P])
                    dve.tensor_tensor(S, S, last, ALU.mult).then_inc(K.sem("state_decayed"), 1)
                    dve.wait_ge(K.sem("state_decayed"), K.count("state_decayed", n + 1))
                    dve.tensor_tensor(S, S, bank(7), ALU.add).then_inc(K.sem("state"), 1)
    K.done(state=1 + 2 * TT, v_fixed=TT, square=TT, summed=TT, logged=TT, rstd=TT, normed=2 * TT, tokens_major=2 * TT,
           g_fixed=TT, row_sums=TT, scores=2 * TT, between=6 * TT, half_turned=6 * TT, half_kept=6 * TT,
           correction=12 * TT, inverse_kept=12 * TT, solved=2 * TT, solved_kept=2 * TT, scaled=3 * TT, recalled=2 * TT,
           v_new=2 * TT, mixed=2 * TT, o_ready=2 * TT, learnt=2 * TT, d_ready=2 * TT, d_pos=TT, decay=2 * TT,
           row_decay=TT, a_beta=TT, a_ready=TT, masked=TT, qk_ready=TT, q_decayed=TT, state_decayed=2 * TT)


def rope(K, x, n, base):
    nc = K.nc
    ang, red, cos, sin, t0 = (K.big(base + m * T, T) for m in range(5))
    ki = K.big(base + 5 * T, T).bitcast(I32)
    kf, t1, t2 = (K.big(base + (6 + m) * T, T) for m in range(3))
    posi = K.big(base + 9 * T, T).bitcast(I32)
    c1, c2 = 6.28125, float(np.float32(2 * np.pi - 6.28125 - 0.0) // np.float32(2 ** -20) * 2 ** -20)
    c3 = float(2 * np.pi - c1 - c2)
    with nc.Block() as block:
        @block.sync
        def _(sp):
            sp.dma_start(posi, K.ins["pos"].broadcast_to([P, T])).then_inc(K.sem("loaded"), 16)

        @block.vector
        def _(dve):
            step = 0

            def then(ins):
                nonlocal step
                step += 1
                ins.then_inc(K.sem("step_dve"), 1)
                dve.wait_ge(K.sem("step_dve"), K.count("step_dve", step))
            dve.wait_ge(K.sem("loaded"), K.count("loaded", 16))
            then(dve.tensor_copy(kf, posi))
            then(dve.tensor_scalar(ang, kf, K.c("invfreq"), None, ALU.mult))
            for phase, dst in ((0.0, sin), (0.25, cos)):
                then(dve.tensor_scalar(kf, ang, 1.0 / (2 * np.pi), phase, ALU.mult, ALU.add))
                then(dve.tensor_copy(ki, kf))
                then(dve.tensor_copy(kf, ki))
                then(dve.scalar_tensor_tensor(red, kf, -c1, ang, ALU.mult, ALU.add))
                then(dve.scalar_tensor_tensor(red, kf, -c2, red, ALU.mult, ALU.add))
                then(dve.scalar_tensor_tensor(red, kf, -c3, red, ALU.mult, ALU.add))
                then(dve.tensor_scalar(red, red, phase * 2 * np.pi, None, ALU.add))
                then(dve.tensor_scalar(t0, red, float(np.float32(np.pi)), -2 * np.pi, ALU.is_gt, ALU.mult))
                then(dve.tensor_tensor(red, red, t0, ALU.add))
                then(dve.tensor_scalar(t0, red, -float(np.float32(np.pi)), 2 * np.pi, ALU.is_lt, ALU.mult))
                then(dve.tensor_tensor(red, red, t0, ALU.add))
                then(dve.tensor_scalar(dst, red, 3.1415925, -3.1415925, ALU.min, ALU.max))
            with dve.Fori(0, n) as i:
                dve.wait_ge(K.sem("step_act"), K.count("step_act", 2))
                dve.wait_ge(K.sem("product"), K.count("product", i + 1))
                dve.wait_ge(K.sem("rotated"), K.count("rotated", i))
                at = x[:, ds(i * T, T)]
                dve.tensor_tensor(t1, K.ps[:, 0, :], sin, ALU.mult).then_inc(K.sem("taken_dve"), 1)
                dve.tensor_tensor(t2, at, cos, ALU.mult).then_inc(K.sem("gated"), 1)
                dve.wait_ge(K.sem("taken_dve"), K.count("taken_dve", i + 1))
                dve.wait_ge(K.sem("gated"), K.count("gated", i + 1))
                dve.tensor_tensor(at, t1, t2, ALU.add).then_inc(K.sem("rotated"), 1)

        @block.scalar
        def _(act):
            act.wait_ge(K.sem("step_dve"), K.count("step_dve", 26))
            act.activation(sin, sin, ACT.Sin).then_inc(K.sem("step_act"), 1)
            act.activation(cos, cos, ACT.Sin).then_inc(K.sem("step_act"), 1)

        @block.tensor
        def _(pe):
            with pe.Fori(0, n) as i:
                pe.wait_ge(K.sem("taken_dve"), K.count("taken_dve", i))
                pe.matmul(K.ps[:, 0, :], K.c("rot"), x[:, ds(i * T, T)], start=True, stop=True)\
                  .then_inc(K.sem("product"), 1)
    K.done(loaded=16, step_dve=26, step_act=2, product=n, taken_dve=n, gated=n, rotated=n)


def lambdas(K, neg_lam, lambda_init):
    nc = K.nc
    v = K.v("lams").rearrange("p (n d) -> p n d", n=4)
    s, t = K.small[:, 84:90], K.big(0, P).rearrange("p (n d) -> p n d", n=2)
    with nc.Block() as block:
        @block.vector
        def _(dve):
            dve.tensor_tensor(t, v[:, 0:4:2, :], v[:, 1:4:2, :], ALU.mult).then_inc(K.sem("step_dve"), 1)
            dve.wait_ge(K.sem("step_dve"), K.count("step_dve", 1))
            dve.tensor_reduce(s[:, 0:2], t, AX, ALU.add).then_inc(K.sem("step_dve"), 1)
            dve.wait_ge(K.sem("step_act"), K.count("step_act", 1))
            dve.tensor_tensor(s[:, 4:5], s[:, 3:4], s[:, 2:3], ALU.subtract).then_inc(K.sem("step_dve"), 1)
            dve.wait_ge(K.sem("step_dve"), K.count("step_dve", 3))
            dve.tensor_scalar(neg_lam, s[:, 4:5], -lambda_init, None, ALU.add)

        @block.scalar
        def _(act):
            act.wait_ge(K.sem("step_dve"), K.count("step_dve", 2))
            act.activation(s[:, 2:4], s[:, 0:2], ACT.Exp).then_inc(K.sem("step_act"), 1)
    K.done(step_dve=3, step_act=1)


def even_mixer(K):
    raw, z, vb, conv = K.big(0, 20 * T), K.big(20 * T, 4 * T), K.big(24 * T, 4 * T), K.big(28 * T, 12 * T)
    G, BETA, GC, BG, KDF = (K.small[:, 16 * n:16 * n + 16] for n in range(5))
    neg_lam = K.small[:, 99:100]
    linear(K, 5, K.H, copy_to(raw))
    linear(K, 1, K.H, copy_to(z, ACT.Silu), sides=("act",) * 4)
    linear(K, 1, K.H, tokens_to(vb, 512), token_major=True)
    gates(K, G, BETA, GC, BG, KDF)
    short_conv(K, raw, conv, 12)
    mix = K.H.rearrange("p k t -> p (k t)")
    gated_delta_room = 40 * T
    gated_delta(K, conv, mix[:, 0:4 * T], G, BETA, GC, BG, KDF, gated_delta_room)
    head_norm(K, mix[:, 0:4 * T], 4, K.v("gdn_norm"), 1.0, gate=z)
    qb, kb = K.big(12 * T, 4 * T), K.big(16 * T, 4 * T)
    h3 = lambda t: t.rearrange("p (h t) -> p h t", t=T)
    rope(K, K.big(12 * T, 8 * T), 8, 0)
    lambdas(K, neg_lam, 0.2)
    attention(K, 4, 2, h3(qb), h3(kb), vb.rearrange("p (i n) -> p i n", n=512), "scale64",
              h3(mix[:, 4 * T:8 * T]), neg_lam=neg_lam, base=28 * T)
    head_norm(K, mix[:, 4 * T:8 * T], 4, K.v("diff_norm"), 1.0 - 0.2)
    linear(K, 2, K.H, plus_x(K), sides=("dve",) * 4)


def ada(K, layer, dst):
    nc = K.nc
    cs = K.small[:, 0:16].rearrange("p (k n) -> p k n", k=8)
    with nc.Block() as block:
        @block.scalar
        def _(act):
            act.activation(cs, K.v("c_vecs").rearrange("p (k n) -> p k n", k=8), ACT.Silu)
    bias = K.v(f"ada_b{layer}")

    def evac(eng, side, g, j, ps):
        return eng.tensor_scalar(dst[:, ds(g * 8 + j * 2, 2)], ps, bias[:, ds(4 * g + j, 1)], None, ALU.add)
    linear(K, 6, cs, evac, sides=("dve",) * 4, width=2)


def modulation(K, m, gain, scaled, col):
    sc = m.rearrange("p (n c) -> p n c", c=2)[:, 8:16, col]
    with K.nc.Block() as block:
        @block.vector
        def _(dve):
            dve.scalar_tensor_tensor(scaled, sc, 1.0, gain, ALU.add, ALU.mult)


def hgrn(K, base, HC, OH):
    nc = K.nc
    at = base

    def room(n):
        nonlocal at
        at += n
        return K.big(at - n, n)
    ZW = 4 * T + 2 * CTX
    Z = room(2 * ZW).rearrange("p (b n) -> p b n", b=2)
    L = room(ZW)
    B = room(2 * T + 2 * CTX)
    F = room(7 * T + CTX)
    V = room(2 * T).rearrange("p (b i n) -> p b i n", b=2, i=TT)
    VC = room(2 * CTX).rearrange("p (b i n) -> p b i n", b=2, i=2)
    SC = room(2 * T).rearrange("p (d i n) -> p d i n", d=2, i=TT)
    KT = room(T).rearrange("p (i n) -> p i n", i=TT)
    KCT = room(CTX).rearrange("p (i n) -> p i n", i=2)
    S = K.sq[:, 1, :].rearrange("p (i n) -> p i n", i=TT)
    WV = room(2 * 1024).rearrange("p (b k n) -> p b k n", b=2, k=8)
    ends = K.small[:, 0:4]
    LV, DQ, DK, QI, KD_, KC = F[:, 0:3 * T], F[:, 3 * T:4 * T], F[:, 4 * T:5 * T], F[:, 5 * T:6 * T], \
        F[:, 6 * T:7 * T], F[:, 7 * T:7 * T + CTX]
    wv_landed = [K.landed_v[0], K.landed_v[1]]
    zc = lambda n, w=T: slice(n, n + w)
    zq, zg, zk, zkc = zc(0), zc(T), (zc(2 * T), zc(3 * T)), (zc(4 * T, CTX), zc(4 * T + CTX, CTX))
    bs = (B[:, 0:T], B[:, T:2 * T])
    bc = (B[:, 2 * T:2 * T + CTX], B[:, 2 * T + CTX:])
    i4 = lambda a: a.rearrange("p (i n) -> p i n", n=P)
    kinds = (("diag_f", "up4", "up5", "up6"), ("diag_b", "low4", "low5", "low6"))
    first = K.tile

    def steps(eng, step):
        step(0, 0, None, 0)
        with eng.Fori(0, HG // 2 - 1) as r:
            step(r, 2 * r + 1, 2 * r, 1)
            step(r + 1, 2 * r + 2, 2 * r + 1, 0)
        step(HG // 2 - 1, HG - 1, HG - 2, 1)
        step(None, None, HG - 1, 0)

    def levels(d):
        for n, z in enumerate((16, 32, 64)):
            b = bs[d].rearrange("p (n two z) -> p n two z", two=2, z=z)
            f = LV[:, n * T:(n + 1) * T].rearrange("p (n two z) -> p n two z", two=2, z=z)
            later, earlier = (1, 0) if d == 0 else (0, 1)
            mid = b[:, :, 0, z - 1:z] if d == 0 else b[:, :, 1, 0:1]
            yield z, n, b, f, later, earlier, mid.broadcast_to([P, T // (2 * z), z])

    with nc.Block() as block:
        @block.sync
        def _(sp):
            for s in range(2):
                sp.dma_start(WV[:, s].rearrange("p k n -> p (k n)"), K.ins["wv"][s, :, :]).then_inc(wv_landed[s], 16)
            def one(g, r, off, slot):
                sp.wait_ge(K.sem("product"), K.count("product", 7 * (g + 1)))
                sp.dma_start(K.W[:, slot, :], K.wstream[ds(first + 2 + g, 1), :, :].rearrange("g p n -> p (g n)"))\
                  .then_inc(K.landed[slot], 16)

            def values(g, s):
                sp.dma_start(WV[:, s].rearrange("p k n -> p (k n)"),
                             K.ins["wv"][ds(g + 2, 1), :, :].rearrange("g p n -> p (g n)")).then_inc(wv_landed[s], 16)
            with sp.Fori(0, HG // 2 - 1) as r:
                for off in range(2):
                    one(2 * r + off, r, off, (first + off) % 2)
                    values(2 * r + off, off)
            for g in range(HG - 2, HG):
                if first + 2 + g < K.ntiles:
                    one(g, 0, g, (first + g) % 2)

        @block.tensor
        def _(pe):
            def project(bank, lo, w, col, src, width):
                for k in range(8):
                    mm = pe.matmul(K.ps[:, bank, lo:lo + width], w[:, k, col * P:(col + 1) * P], src[:, k, 0:width],
                                   start=(k == 0), stop=(k == 7), skip_group_check=True)
                return mm

            def recur(p, d, par):
                m = 2 * p + d
                v, vc = V[:, par], VC[:, par]
                pe.wait_ge(K.sem("k_decayed"), K.count("k_decayed", m + 1))
                pe.wait_ge(K.sem("states"), K.count("states", m))
                for j in range(2):
                    mm = pe.transpose(K.ps[:, 7, j * P:(j + 1) * P], KC[:, j * P:(j + 1) * P], K.c("ident"))
                mm.then_inc(K.sem("ctx_turned"), 1)

                def scores(kind):
                    bank = K.ps[:, 4 + kind % 2, :]
                    for i in range(TT):
                        s = slice(i * P, (i + 1) * P)
                        l, r = (DK, DQ) if kind == 0 else (LV[:, (kind - 1) * T:kind * T],) * 2
                        mm = pe.matmul(bank[:, s], l[:, s], r[:, s], start=True, stop=True)
                    mm.then_inc(K.sem("scores"), 1)
                pe.wait_ge(K.sem("diag_ready"), K.count("diag_ready", m + 1))
                pe.wait_ge(K.sem("sc_kept"), K.count("sc_kept", 4 * m))
                pe.wait_ge(K.sem("logged"), K.count("logged", p))
                scores(0)
                pe.wait_ge(K.sem("levels_ready"), K.count("levels_ready", m + 1))
                scores(1)
                pe.wait_ge(K.sem("kct_kept"), K.count("kct_kept", m + 1))
                for i in range(TT):
                    mm = pe.transpose(K.ps[:, 7, i * P:(i + 1) * P], KD_[:, i * P:(i + 1) * P], K.c("ident"))
                mm.then_inc(K.sem("turned"), 1)
                pe.wait_ge(K.sem("sc_kept"), K.count("sc_kept", 4 * m + 1))
                scores(2)
                pe.wait_ge(K.sem("sc_kept"), K.count("sc_kept", 4 * m + 2))
                scores(3)
                pe.wait_ge(K.sem("evac_dve"), K.count("evac_dve", 2 * (p + 1)))
                for j in range(2):
                    mm = pe.matmul(K.ps[:, 3, 0:P], KCT[:, j, :], vc[:, j, :], start=(j == 0), stop=(j == 1))
                mm.then_inc(K.sem("ctx_state"), 1)
                pe.wait_ge(K.sem("kt_kept"), K.count("kt_kept", m + 1))
                for i in range(TT):
                    mm = pe.matmul(K.ps[:, 7, i * P:(i + 1) * P], KT[:, i, :], v[:, i, :], start=True, stop=True)
                mm.then_inc(K.sem("learnt"), 1)
                pe.wait_ge(K.sem("sc_kept"), K.count("sc_kept", 4 * m + 4))
                pe.wait_ge(K.sem("q_decayed"), K.count("q_decayed", m + 1))
                pe.wait_ge(K.sem("states"), K.count("states", m + 1))
                if d == 0:
                    pe.wait_ge(K.sem("o_taken"), K.count("o_taken", p))
                for i in range(TT):
                    o = K.ps[:, 6, i * P:(i + 1) * P]
                    pe.matmul(o, v[:, i, :], SC[:, d, i, :], start=(i == 0 and d == 0), stop=False,
                              skip_group_check=True)
                    mm = pe.matmul(o, S[:, i, :], QI[:, i * P:(i + 1) * P], start=False, stop=(d == 1),
                                   skip_group_check=True)
                mm.then_inc(K.sem("mixed"), 1)

            def step(hr, h, p, par):
                if h is not None:
                    slot = (first + par) % 2
                    w = K.W[:, slot, :].rearrange("p (k n) -> p k n", k=8)
                    pe.wait_ge(K.landed[slot], 16 * ((first + par) // 2 + 1) + 16 * hr)
                    pe.wait_ge(K.sem("evac_act"), K.count("evac_act", 5 * h))
                    project(0, 0, w, 0, K.H, T).then_inc(K.sem("product"), 1)
                    pe.wait_ge(K.sem("evac_dve"), K.count("evac_dve", 2 * h - 1))
                    project(1, 0, w, 1, K.H, T).then_inc(K.sem("product"), 1)
                if p is not None:
                    pe.wait_ge(K.sem("evac_act"), K.count("evac_act", 5 * p + 4))
                    recur(p, 0, 1 - par)
                if h is not None:
                    pe.wait_ge(K.sem("evac_dve"), K.count("evac_dve", 2 * h))
                    project(2, 0, w, 2, K.H, T).then_inc(K.sem("product"), 1)
                    if p is not None:
                        pe.wait_ge(K.sem("s0_kept"), K.count("s0_kept", 2 * p + 1))
                    project(3, 0, w, 3, K.H, T).then_inc(K.sem("product"), 1)
                    pe.wait_ge(K.sem("evac_act"), K.count("evac_act", 5 * h + 1))
                    project(0, 0, w, 2, HC, CTX)
                    project(0, CTX, w, 3, HC, CTX).then_inc(K.sem("product"), 1)
                    pe.wait_ge(K.sem("evac_act"), K.count("evac_act", 5 * h + 2))
                    pe.wait_ge(wv_landed[par], 16 + 16 * hr)
                    for i in range(TT):
                        for k in range(8):
                            mm = pe.matmul(K.ps[:, 1, i * P:(i + 1) * P], K.H[:, k, i * P:(i + 1) * P], WV[:, par, k, :],
                                           start=(k == 0), stop=(k == 7), skip_group_check=True)
                    mm.then_inc(K.sem("product"), 1)
                    pe.wait_ge(K.sem("evac_act"), K.count("evac_act", 5 * h + 3))
                    for i in range(2):
                        for k in range(8):
                            mm = pe.matmul(K.ps[:, 2, i * P:(i + 1) * P], HC[:, k, i * P:(i + 1) * P], WV[:, par, k, :],
                                           start=(k == 0), stop=(k == 7), skip_group_check=True)
                    mm.then_inc(K.sem("product"), 1)
                    pe.wait_ge(K.sem("evac_act"), K.count("evac_act", 5 * h + 4))
                if p is not None:
                    recur(p, 1, 1 - par)
                    pe.wait_ge(K.sem("square"), K.count("square", p + 1))
                    pe.matmul(K.ps[:, 4, :], K.c("ones"), K.sq[:, 0, :], start=True, stop=True)\
                      .then_inc(K.sem("summed"), 1)
            steps(pe, step)

        @block.scalar
        def _(act):
            def exps(p, d):
                m = 2 * p + d
                act.wait_ge(K.sem("args"), K.count("args", m + 1))
                act.activation(DK, DQ, ACT.Exp, scale=-1.0).then_inc(K.sem("dk_exp"), 1)
                act.wait_ge(K.sem("dk_exp"), K.count("dk_exp", m + 1))
                act.activation(F[:, 0:4 * T], F[:, 0:4 * T], ACT.Exp).then_inc(K.sem("exp_levels"), 1)
                act.activation(F[:, 6 * T:7 * T + CTX], F[:, 6 * T:7 * T + CTX], ACT.Exp)
                end = slice(P - 1, P) if d == 0 else slice(0, 1)
                act.activation(ends, i4(bs[d])[:, :, end].rearrange("p i o -> p (i o)"), ACT.Exp)
                act.activation(QI, bs[d], ACT.Exp).then_inc(K.sem("exp_rest"), 1)

            def keep(p, d):
                m = 2 * p + d
                act.wait_ge(K.sem("ctx_turned"), K.count("ctx_turned", m + 1))
                act.activation(KCT.rearrange("p i n -> p (i n)"), K.ps[:, 7, 0:CTX], ACT.Copy)\
                   .then_inc(K.sem("kct_kept"), 1)
                act.wait_ge(K.sem("turned"), K.count("turned", m + 1))
                act.activation(KT.rearrange("p i n -> p (i n)"), K.ps[:, 7, :], ACT.Copy).then_inc(K.sem("kt_kept"), 1)

            def take(h, par, n):
                act.wait_ge(K.sem("product"), K.count("product", 7 * h + n + 1))
                act.activation(Z[:, par, n * T:(n + 1) * T], K.ps[:, n % 4, :], ACT.Copy).then_inc(K.sem("evac_act"), 1)

            def step(hr, h, p, par):
                if p is not None:
                    exps(p, 0)
                if h is not None:
                    act.wait_ge(K.sem("head_out"), K.count("head_out", h - 1))
                    take(h, par, 0)
                    take(h, par, 1)
                if p is not None:
                    keep(p, 0)
                    exps(p, 1)
                if h is not None:
                    take(h, par, 2)
                    take(h, par, 3)
                    take(h, par, 4)
                if p is not None:
                    keep(p, 1)
                    act.wait_ge(K.sem("mixed"), K.count("mixed", 2 * p + 2))
                    act.activation(K.sq[:, 0, :], K.ps[:, 6, :], ACT.Square).then_inc(K.sem("square"), 1)
                    act.wait_ge(K.sem("summed"), K.count("summed", p + 1))
                    act.activation(K.ln[:, :], K.ps[:, 4, :], ACT.Ln, scale=1.0 / P, bias=K.c("eps"))\
                       .then_inc(K.sem("logged"), 1)
                    act.wait_ge(K.sem("logged"), K.count("logged", p + 1))
                    act.wait_ge(K.sem("o_taken"), K.count("o_taken", p))
                    act.activation(K.rstd[:, :], K.ln[:, :], ACT.Exp, scale=-0.5).then_inc(K.sem("rstd"), 1)
                if h is not None:
                    act.wait_ge(K.sem("evac_act"), K.count("evac_act", 5 * h + 5))
                    act.wait_ge(K.sem("logsig"), K.count("logsig", 7 * h))
                    act.activation(L, Z[:, par, :], ACT.Abs).then_inc(K.sem("softplus"), 1)
                    act.wait_ge(K.sem("softplus"), K.count("softplus", 5 * h + 1))
                    act.activation(L, L, ACT.Exp, scale=-1.0).then_inc(K.sem("softplus"), 1)
                    act.wait_ge(K.sem("softplus"), K.count("softplus", 5 * h + 2))
                    act.activation(L, L, ACT.Ln, bias=1.0).then_inc(K.sem("softplus"), 1)
                    act.wait_ge(K.sem("logsig"), K.count("logsig", 7 * h + 2))
                    act.activation(L[:, 0:2 * T], L[:, 0:2 * T], ACT.Exp).then_inc(K.sem("softplus"), 1)
                    act.activation(Z[:, par, 2 * T:], Z[:, par, 2 * T:], ACT.Exp).then_inc(K.sem("softplus"), 1)
            steps(act, step)

        @block.gpsimd
        def _(pool):
            pool.memset(SC, 0.0).then_inc(K.sem("step_pool"), 1)

            def step(hr, h, p, par):
                if p is None:
                    return
                z = Z[:, 1 - par]
                for d in range(2):
                    m = 2 * p + d
                    pool.wait_ge(K.sem("exp_levels"), K.count("exp_levels", m + 1))
                    pool.wait_ge(K.sem("logsig"), K.count("logsig", 7 * p + 7))
                    pool.wait_ge(K.sem("softplus"), K.count("softplus", 5 * p + 5))
                    for s, n, b, f, later, earlier, mid in levels(d):
                        v = lambda c, half: z[:, c].rearrange("p (n two z) -> p n two z", two=2, z=s)[:, :, half, :]
                        pool.tensor_tensor(f[:, :, later, :], f[:, :, later, :], v(zq, later), ALU.mult)
                        mm = pool.tensor_tensor(f[:, :, earlier, :], f[:, :, earlier, :], v(zk[d], earlier), ALU.mult)
                    mm.then_inc(K.sem("levels_ready"), 1)
            steps(pool, step)

        @block.vector
        def _(dve):
            def arguments(p, d):
                m = 2 * p + d
                b, c = bs[d], bc[d]
                dve.wait_ge(K.sem("logsig"), K.count("logsig", 7 * p + 6))
                dve.wait_ge(K.sem("mixed"), K.count("mixed", m))
                for s, n, bb, f, later, earlier, mid in levels(d):
                    dve.tensor_tensor(f[:, :, later, :], bb[:, :, later, :], mid, ALU.subtract)
                    dve.tensor_tensor(f[:, :, earlier, :], mid, bb[:, :, earlier, :], ALU.subtract)
                w = b.rearrange("p (n z) -> p n z", z=16)
                ref = w[:, :, 8:9] if d == 0 else w[:, :, 7:8]
                dve.tensor_tensor(DQ.rearrange("p (n z) -> p n z", z=16), w, ref.broadcast_to([P, T // 16, 16]),
                                  ALU.subtract)
                end = i4(b)[:, :, P - 1:P] if d == 0 else i4(b)[:, :, 0:1]
                dve.tensor_tensor(i4(KD_), end.broadcast_to([P, TT, P]), i4(b), ALU.subtract)
                end = c[:, CTX - 1:CTX] if d == 0 else c[:, 0:1]
                dve.tensor_tensor(KC, end.broadcast_to([P, CTX]), c, ALU.subtract).then_inc(K.sem("args"), 1)

            def factors(p, d, z):
                m = 2 * p + d
                dve.wait_ge(K.sem("exp_rest"), K.count("exp_rest", m + 1))
                dve.wait_ge(K.sem("softplus"), K.count("softplus", 5 * p + 5))
                dve.wait_ge(K.sem("logsig"), K.count("logsig", 7 * p + 7))
                dve.tensor_tensor(KD_, KD_, z[:, zk[d]], ALU.mult)
                dve.tensor_tensor(KC, KC, z[:, zkc[d]], ALU.mult).then_inc(K.sem("k_decayed"), 1)
                dve.tensor_tensor(DQ, DQ, z[:, zq], ALU.mult)
                dve.tensor_tensor(DK, DK, z[:, zk[d]], ALU.mult).then_inc(K.sem("diag_ready"), 1)
                dve.tensor_tensor(QI, QI, z[:, zq], ALU.mult).then_inc(K.sem("q_decayed"), 1)

            def recur(p, d):
                m = 2 * p + d
                dve.wait_ge(K.sem("step_pool"), K.count("step_pool", 1))
                dve.wait_ge(K.sem("mixed"), K.count("mixed", m - 1))
                for kind in range(4):
                    dve.wait_ge(K.sem("scores"), K.count("scores", 4 * m + kind + 1))
                    dve.wait_ge(K.sem("sc_kept"), K.count("sc_kept", 4 * m + kind))
                    K.apart(dve)
                    mask = K.c(kinds[d][kind]).bitcast(I32).unsqueeze(1).broadcast_to([P, TT, P])
                    dve.copy_predicated(SC[:, d], mask, i4(K.ps[:, 4 + kind % 2, :])).then_inc(K.sem("sc_kept"), 1)
                order = (0, 1, 2, 3) if d == 0 else (3, 2, 1, 0)
                dve.wait_ge(K.sem("ctx_state"), K.count("ctx_state", m + 1))
                dve.tensor_copy(S[:, order[0], :], K.ps[:, 3, 0:P]).then_inc(K.sem("s0_kept"), 1)
                dve.wait_ge(K.sem("learnt"), K.count("learnt", m + 1))
                dve.wait_ge(K.sem("s0_kept"), K.count("s0_kept", m + 1))
                for n in range(3):
                    a, b = order[n], order[n + 1]
                    if n:
                        dve.wait_ge(K.sem("chain"), K.count("chain", 2 * m + n))
                    ins = dve.scalar_tensor_tensor(S[:, b, :], S[:, a, :], ends[:, a:a + 1],
                                                   K.ps[:, 7, a * P:(a + 1) * P], ALU.mult, ALU.add)
                    ins.then_inc(K.sem("chain" if n < 2 else "states"), 1)

            def step(hr, h, p, par):
                if p is not None:
                    z = Z[:, 1 - par]
                    for d in range(2):
                        arguments(p, d)
                        factors(p, d, z)
                        recur(p, d)
                    dve.wait_ge(K.sem("rstd"), K.count("rstd", p + 1))
                    o = OH[:, ds(p * T, T)]
                    dve.scalar_tensor_tensor(o, K.ps[:, 6, :], K.v("hgrn_norm"), K.rstd[:, :], ALU.mult, ALU.mult)\
                       .then_inc(K.sem("o_taken"), 1)
                    dve.wait_ge(K.sem("o_taken"), K.count("o_taken", p + 1))
                    dve.tensor_tensor(o, o, z[:, zg], ALU.mult).then_inc(K.sem("head_out"), 1)
                if h is not None:
                    dve.wait_ge(K.sem("mixed"), K.count("mixed", 2 * h - 2))
                    dve.wait_ge(K.sem("product"), K.count("product", 7 * h + 6))
                    dve.tensor_copy(V[:, par].rearrange("p i n -> p (i n)"), K.ps[:, 1, :])\
                       .then_inc(K.sem("evac_dve"), 1)
                    dve.wait_ge(K.sem("product"), K.count("product", 7 * h + 7))
                    dve.tensor_copy(VC[:, par].rearrange("p i n -> p (i n)"), K.ps[:, 2, 0:CTX])\
                       .then_inc(K.sem("evac_dve"), 1)
                    dve.wait_ge(K.sem("softplus"), K.count("softplus", 5 * h + 3))
                    dve.scalar_tensor_tensor(L, Z[:, par, :], 0.0, L, ALU.min, ALU.subtract)\
                       .then_inc(K.sem("logsig"), 1)
                    dve.wait_ge(K.sem("logsig"), K.count("logsig", 7 * h + 1))
                    dve.tensor_tensor(Z[:, par, 2 * T:], L[:, 2 * T:], Z[:, par, 2 * T:], ALU.subtract)\
                       .then_inc(K.sem("logsig"), 1)
                    dve.wait_ge(K.sem("exp_rest"), K.count("exp_rest", 2 * h))
                    ones = K.c("ones")[:, 0:1].broadcast_to([P, CTX])
                    for d, rev in ((0, False), (1, True)):
                        f = (lambda a: a[:, ::-1]) if rev else (lambda a: a)
                        dve.tensor_tensor_scan(f(bs[d]), f(K.c("resets_b" if rev else "resets_f")),
                                               f(L[:, (2 + d) * T:(3 + d) * T]), 0.0, ALU.mult, ALU.add)\
                           .then_inc(K.sem("logsig"), 1)
                        dve.tensor_tensor_scan(f(bc[d]), ones[:, 0:CTX],
                                               f(L[:, 4 * T + d * CTX:4 * T + (d + 1) * CTX]), 0.0, ALU.mult, ALU.add)\
                           .then_inc(K.sem("logsig"), 1)
                    dve.wait_ge(K.sem("softplus"), K.count("softplus", 5 * h + 4))
                    dve.tensor_tensor(Z[:, par, 0:2 * T], Z[:, par, 0:2 * T], L[:, 0:2 * T], ALU.mult)\
                       .then_inc(K.sem("logsig"), 1)
            steps(dve, step)
    K.done(product=7 * HG, evac_act=5 * HG, evac_dve=2 * HG, k_decayed=2 * HG, states=2 * HG, ctx_turned=2 * HG,
           scores=8 * HG, diag_ready=2 * HG, sc_kept=8 * HG, logged=HG, levels_ready=2 * HG, kct_kept=2 * HG,
           turned=2 * HG, ctx_state=2 * HG, kt_kept=2 * HG, learnt=2 * HG, q_decayed=2 * HG, o_taken=HG,
           mixed=2 * HG, s0_kept=2 * HG, square=HG, summed=HG, args=2 * HG, dk_exp=2 * HG, exp_levels=2 * HG,
           exp_rest=2 * HG, rstd=HG, softplus=5 * HG, logsig=7 * HG, step_pool=1, chain=4 * HG, head_out=HG)
    K.tile += HG


def gated_plus_x(K, m, col):
    x = K.X.rearrange("p k t -> p (k t)")

    def add(dve, n, j, ps):
        at = x[:, ds(n * 2048 + j * 512, 512)]
        return dve.scalar_tensor_tensor(at, ps, m[:, ds((16 + 4 * n + j) * 2 + col, 1)], at, ALU.mult, ALU.add)
    return add


def hgrn_layer(K):
    m = K.mod
    ada(K, 0, m)
    gx, gc = K.small[:, 16:24], K.small[:, 24:32]
    modulation(K, m, K.v("norm_g0"), gx, 0)
    modulation(K, m, K.v("norm_g0"), gc, 1)
    shift = m.rearrange("p (n c) -> p n c", c=2)
    OH = K.big(0, 16 * T)
    HC = K.big(16 * T, 8 * CTX).rearrange("p (k t) -> p k t", k=8)
    with K.nc.Block() as block:
        @block.sync
        def _(sp):
            sp.dma_start(HC, K.ins["ctxT"]).then_inc(K.sem("loaded"), 16)
            sp.wait_ge(K.sem("loaded"), K.count("loaded", 16))
    K.done(loaded=16)
    norm(K, HC, HC, gc, width=CTX, shift=shift[:, 0:8, 1])
    norm(K, K.X, K.H, gx, shift=shift[:, 0:8, 0])
    hgrn(K, 16 * T + 8 * CTX, HC, OH)
    linear_deep(K, 2, tiles_in(OH), 8, gated_plus_x(K, m, 0))


def layer_stats(K, x, tiles, mean_of, eps_col, y_mean):
    nc = K.nc
    n = tiles
    with nc.Block() as block:
        @block.tensor
        def _(pe):
            for k in range(n):
                mm = pe.matmul(K.ps[:, 0, :], K.c("ones"), x[:, k * T:(k + 1) * T], start=(k == 0), stop=(k == n - 1))
            mm.then_inc(K.sem("summed"), 1)
            for k in range(n):
                pe.wait_ge(K.sem("square"), K.count("square", k + 1))
                pe.matmul(K.ps[:, 1, :], K.c("ones"), K.sq[:, k % 2, :], start=(k == 0), stop=(k == n - 1))\
                  .then_inc(K.sem("summed"), 1)

        @block.vector
        def _(dve):
            dve.wait_ge(K.sem("summed"), K.count("summed", 1))
            dve.tensor_scalar(y_mean, K.ps[:, 0, :], 1.0 / mean_of, None, ALU.mult).then_inc(K.sem("step_dve"), 1)
            dve.wait_ge(K.sem("step_dve"), K.count("step_dve", 1))
            for k in range(n):
                at = x[:, k * T:(k + 1) * T]
                dve.tensor_tensor(at, at, y_mean, ALU.subtract).then_inc(K.sem("centered"), 1)

        @block.scalar
        def _(act):
            for k in range(n):
                act.wait_ge(K.sem("centered"), K.count("centered", k + 1))
                act.wait_ge(K.sem("summed"), K.count("summed", k))
                act.activation(K.sq[:, k % 2, :], x[:, k * T:(k + 1) * T], ACT.Square).then_inc(K.sem("square"), 1)
            act.wait_ge(K.sem("summed"), K.count("summed", n + 1))
            act.activation(K.ln[:, :], K.ps[:, 1, :], ACT.Ln, scale=1.0 / mean_of, bias=eps_col)\
               .then_inc(K.sem("logged"), 1)
            act.wait_ge(K.sem("logged"), K.count("logged", 1))
            act.activation(K.rstd[:, :], K.ln[:, :], ACT.Exp, scale=-0.5)
    K.done(summed=n + 1, square=n, centered=n, step_dve=1, logged=1)


def conv_layer(K):
    nc = K.nc
    m = K.mod
    ada(K, 1, m)
    gx, xb = K.small[:, 16:24], K.small[:, 24:32]
    modulation(K, m, K.v("norm_g1"), gx, 0)
    shift = m.rearrange("p (n c) -> p n c", c=2)
    norm(K, K.X, K.H, gx, shift=shift[:, 0:8, 0])
    Y, Zg = K.big(0, 16 * T), K.big(16 * T, 16 * T)
    U = K.big(32 * T, 8 * T).rearrange("p (b n) -> p b n", b=2)
    taps, bin_, dwb = K.v("conv_dw"), K.v("conv_b_in"), K.v("conv_dw_b")
    first = K.tile
    with nc.Block() as block:
        @block.sync
        def _(sp):
            prefetch(K, sp, 12, lambda g: sp.wait_ge(K.sem("product"), K.count("product", 4 * (g + 1))))

        @block.tensor
        def _(pe):
            def one(g, r, off, slot):
                wait_tile(K, pe, r, off, slot)
                if isinstance(g, int) and g >= 10:
                    pe.wait_ge(K.sem("taken_gate"), K.count("taken_gate", 4 * g - 36))
                else:
                    pe.wait_ge(K.sem("taken_dve"), K.count("taken_dve", 2 * g - 2))
                    pe.wait_ge(K.sem("taken_act"), K.count("taken_act", 2 * g - 2))
                w = K.W[:, slot, :].rearrange("p (k n) -> p k n", k=8)
                for j in range(4):
                    for k in range(8):
                        mm = pe.matmul(K.ps[:, 4 * slot + j, :], w[:, k, j * P:(j + 1) * P], K.H[:, k, :],
                                       start=(k == 0), stop=(k == 7))
                    mm.then_inc(K.sem("product"), 1)
            tiles(K, pe, 8, one)
            for g in range(8, 12):
                one(g, 0, g, (first + g) % 2)

        @block.scalar
        def _(act):
            def one(g, r, off, slot):
                b = off % 2
                act.wait_ge(K.sem("glu"), K.count("glu", 2 * g - 2))
                for j in (2, 3):
                    act.wait_ge(K.sem("product"), K.count("product", 4 * g + j + 1))
                    act.activation(U[:, b, j * T:(j + 1) * T], K.ps[:, 4 * slot + j, :], ACT.Sigmoid,
                                   bias=bin_[:, ds(4 * g + j, 1)]).then_inc(K.sem("taken_act"), 1)
            tiles(K, act, 8, one)
            for g in range(8, 12):
                slot = (first + g) % 2
                for j in range(4):
                    act.wait_ge(K.sem("product"), K.count("product", 4 * g + j + 1))
                    act.activation(Zg[:, (4 * (g - 8) + j) * T:(4 * (g - 8) + j + 1) * T], K.ps[:, 4 * slot + j, :],
                                   ACT.Silu, bias=bin_[:, 4 * g + j:4 * g + j + 1])\
                       .then_inc(K.sem("taken_gate"), 1)

        @block.vector
        def _(dve):
            rows8 = lambda a: a.rearrange("p (n w) -> p n w", w=64)

            def one(g, r, off, slot):
                b = off % 2
                for j in (0, 1):
                    dve.wait_ge(K.sem("product"), K.count("product", 4 * g + j + 1))
                    dve.wait_ge(K.sem("glu"), K.count("glu", 2 * g - 2))
                    dve.wait_ge(K.sem("tapped"), K.count("tapped", 62 * g - 2))
                    dve.tensor_scalar(U[:, b, j * T:(j + 1) * T], K.ps[:, 4 * slot + j, :],
                                      bin_[:, ds(4 * g + j, 1)], None, ALU.add).then_inc(K.sem("taken_dve"), 1)
                for j in (0, 1):
                    dve.wait_ge(K.sem("taken_act"), K.count("taken_act", 2 * g + j + 1))
                    dve.wait_ge(K.sem("taken_dve"), K.count("taken_dve", 2 * g + j + 1))
                    u = U[:, b, j * T:(j + 1) * T]
                    dve.tensor_tensor(u, u, U[:, b, (j + 2) * T:(j + 3) * T], ALU.mult).then_inc(K.sem("glu"), 1)
                order = [15] + [i for i in range(31) if i != 15]
                for n, i in enumerate(order):
                    o = i - 15
                    lo, hi = max(0, -o), min(64, 64 - o)
                    for j in (0, 1):
                        u = rows8(U[:, b, j * T:(j + 1) * T])[:, :, lo + o:hi + o]
                        y = rows8(Y[:, ds(g * 2 * T + j * T, T)])[:, :, lo:hi]
                        w = taps[:, ds(g * 62 + j * 31 + i, 1)]
                        if n == 0:
                            dve.wait_ge(K.sem("glu"), K.count("glu", 2 * g + j + 1))
                            dve.tensor_scalar(y, u, w, dwb[:, ds(2 * g + j, 1)], ALU.mult, ALU.add)\
                               .then_inc(K.sem("tapped"), 1)
                        else:
                            dve.wait_ge(K.sem("tapped"), K.count("tapped", 62 * g + 2 * (n - 1) + j + 1))
                            dve.scalar_tensor_tensor(y, u, w, y, ALU.mult, ALU.add).then_inc(K.sem("tapped"), 1)
            tiles(K, dve, 8, one)
    K.done(product=48, taken_dve=16, taken_act=16, taken_gate=16, glu=16, tapped=62 * 8)
    K.tile += 12
    layer_stats(K, Y, 16, 2048.0, K.c("eps"), K.big(32 * T, T))
    g, b = K.v("conv_ln_g"), K.v("conv_ln_b")
    with nc.Block() as block:
        @block.vector
        def _(dve):
            dve.tensor_tensor(xb, K.v("conv_b_out"), shift[:, 16:24, 0], ALU.mult).then_inc(K.sem("step_dve"), 1)
            with dve.Fori(0, 16) as i:
                at = Y[:, ds(i * T, T)]
                dve.scalar_tensor_tensor(at, at, g[:, ds(i, 1)], K.rstd[:, :], ALU.mult, ALU.mult)\
                   .then_inc(K.sem("scaled"), 1)
            with dve.Fori(0, 16) as i:
                at = Y[:, ds(i * T, T)]
                dve.wait_ge(K.sem("silu"), K.count("silu", i + 1))
                dve.tensor_tensor(at, at, Zg[:, ds(i * T, T)], ALU.mult)
            dve.wait_ge(K.sem("step_dve"), K.count("step_dve", 1))
            for k in range(8):
                dve.tensor_scalar(K.X[:, k, :], K.X[:, k, :], xb[:, k:k + 1], None, ALU.add)

        @block.scalar
        def _(act):
            with act.Fori(0, 16) as i:
                at = Y[:, ds(i * T, T)]
                act.wait_ge(K.sem("scaled"), K.count("scaled", i + 1))
                act.activation(at, at, ACT.Silu, bias=b[:, ds(i, 1)]).then_inc(K.sem("silu"), 1)
    K.done(step_dve=1, scaled=16, silu=16)
    linear_deep(K, 2, tiles_in(Y), 8, gated_plus_x(K, m, 0))


def sgu_layer(K):
    nc = K.nc
    Y = K.big(0, 16 * T)
    YA, YB = Y[:, 0:8 * T], Y[:, 8 * T:]
    BA, ZA = K.big(16 * T, 8 * T), K.big(24 * T, 8 * T)
    V = BA
    tmp = K.big(32 * T, 2 * T)
    at = 34 * T
    WS = K.big(at, 1024).rearrange("p (g n) -> p g n", g=8)
    BS = K.big(at + 1024, 1024).rearrange("p (g n) -> p g n", g=8)
    LG, LB = K.big(at + 2048, 1024), K.big(at + 3072, 1024)
    w3 = K.v("short_w")

    def times(dst):
        def evac(eng, side, g, j, ps):
            a = dst[:, ds(g * 2048 + j * 512, 512)]
            return eng.tensor_tensor(a, ps, a, ALU.mult)
        return evac

    def short(dve, g, j):
        n = 4 * g + j
        s = ds(g * 2048 + j * 512, 512)
        a = tmp[:, 0:T]
        dve.wait_ge(K.sem("followed"), K.count("followed", n))
        col = lambda i: w3[:, ds(3 * n + i, 1)]
        dve.tensor_scalar(a, YA[:, s], col(1), None, ALU.mult).then_inc(K.sem("short"), 1)
        dve.wait_ge(K.sem("short"), K.count("short", 4 * n + 1))
        dve.scalar_tensor_tensor(a[:, 1:T], YA[:, ds(g * 2048 + j * 512, 511)], col(0), a[:, 1:T], ALU.mult, ALU.add)\
           .then_inc(K.sem("short"), 1)
        dve.wait_ge(K.sem("short"), K.count("short", 4 * n + 2))
        dve.scalar_tensor_tensor(a[:, 0:T - 1], YA[:, ds(g * 2048 + j * 512 + 1, 511)], col(2), a[:, 0:T - 1],
                                 ALU.mult, ALU.add).then_inc(K.sem("short"), 1)
        dve.wait_ge(K.sem("short"), K.count("short", 4 * n + 3))
        dve.tensor_tensor(a, a, BA[:, s], ALU.mult).then_inc(K.sem("short"), 1)
        dve.wait_ge(K.sem("short"), K.count("short", 4 * n + 4))
        dve.tensor_tensor(YA[:, s], a, ZA[:, s], ALU.mult).then_inc(K.sem("followed"), 1)

    linear(K, 2, K.H, copy_to(YA))
    linear(K, 2, K.H, times(YA), sides=("dve",) * 4)
    linear(K, 2, K.H, copy_to(BA))
    linear(K, 2, K.H, copy_to(ZA, ACT.Silu), sides=("act",) * 4, follow=short)
    K.done(short=32)
    linear(K, 2, K.H, copy_to(YB))
    linear(K, 2, K.H, copy_to(ZA, ACT.Silu), sides=("act",) * 4)
    linear(K, 2, K.H, tokens_to(V, 1024), token_major=True)
    st, mv, lr = K.small[:, 0:48], K.small[:, 48:56], K.small[:, 56:64]
    with nc.Block() as block:
        @block.sync
        def _(sp):
            sp.dma_start(WS, K.ins["sgu_w"]).then_inc(K.sem("loaded"), 16)
            sp.dma_start(BS, K.ins["sgu_b"].broadcast_to([P, 1024])).then_inc(K.sem("loaded"), 16)
            sp.dma_start(LG, K.ins["sgu_ln_g"].broadcast_to([P, 1024])).then_inc(K.sem("loaded"), 16)
            sp.dma_start(LB, K.ins["sgu_ln_b"].broadcast_to([P, 1024])).then_inc(K.sem("loaded"), 16)

        @block.vector
        def _(dve):
            for i in range(TT):
                for n in range(2):
                    dve.bn_stats(st[:, 12 * i + 6 * n:12 * i + 6 * n + 6], V[:, i * 1024 + n * 512:i * 1024 + (n + 1) * 512])\
                       .then_inc(K.sem("stats"), 1)
                dve.wait_ge(K.sem("stats"), K.count("stats", 2 * i + 2))
                dve.bn_aggr(mv[:, 2 * i:2 * i + 2], st[:, 12 * i:12 * i + 12]).then_inc(K.sem("moments"), 1)
            dve.wait_ge(K.sem("step_act"), K.count("step_act", 2))
            dve.wait_ge(K.sem("loaded"), K.count("loaded", 64))
            dve.wait_ge(K.sem("moments"), K.count("moments", TT))
            for i in range(TT):
                v = V[:, i * 1024:(i + 1) * 1024]
                dve.tensor_scalar(v, v, mv[:, 2 * i:2 * i + 1], lr[:, 4 + i:5 + i], ALU.subtract, ALU.mult)\
                   .then_inc(K.sem("step_dve"), 1)
                dve.wait_ge(K.sem("step_dve"), K.count("step_dve", 3 * i + 1))
                dve.tensor_tensor(v, v, LG, ALU.mult).then_inc(K.sem("step_dve"), 1)
                dve.wait_ge(K.sem("step_dve"), K.count("step_dve", 3 * i + 2))
                dve.tensor_tensor(v, v, LB, ALU.add).then_inc(K.sem("step_dve"), 1)
            for g in range(8):
                s = slice(g * T, (g + 1) * T)
                t = tmp[:, (g % 2) * T:(g % 2 + 1) * T]
                dve.wait_ge(K.sem("mixed"), K.count("mixed", g + 1))
                if g == 0:
                    dve.wait_ge(K.sem("gated"), K.count("gated", 8))
                dve.wait_ge(K.sem("followed"), K.count("followed", g - 1))
                dve.tensor_tensor(t.rearrange("p (i n) -> p i n", n=P), K.ps[:, g % 4, :].rearrange("p (i n) -> p i n", n=P),
                                  BS[:, g, :].unsqueeze(1).broadcast_to([P, TT, P]), ALU.add)\
                   .then_inc(K.sem("taken_dve"), 1)
                dve.wait_ge(K.sem("taken_dve"), K.count("taken_dve", g + 1))
                dve.tensor_tensor(YB[:, s], YB[:, s], t, ALU.mult).then_inc(K.sem("followed"), 1)

        @block.gpsimd
        def _(pool):
            for g in range(8):
                s = slice(g * T, (g + 1) * T)
                pool.tensor_tensor(YB[:, s], YB[:, s], ZA[:, s], ALU.mult).then_inc(K.sem("gated"), 1)

        @block.scalar
        def _(act):
            act.wait_ge(K.sem("moments"), K.count("moments", TT))
            act.activation(lr[:, 0:4], mv[:, 1:8:2], ACT.Ln, bias=K.c("eps5")).then_inc(K.sem("step_act"), 1)
            act.wait_ge(K.sem("step_act"), K.count("step_act", 1))
            act.activation(lr[:, 4:8], lr[:, 0:4], ACT.Exp, scale=-0.5).then_inc(K.sem("step_act"), 1)

        @block.tensor
        def _(pe):
            pe.wait_ge(K.sem("step_dve"), K.count("step_dve", 12))
            for g in range(8):
                pe.wait_ge(K.sem("taken_dve"), K.count("taken_dve", g - 3))
                for i in range(TT):
                    mm = pe.matmul(K.ps[:, g % 4, i * P:(i + 1) * P], V[:, i * 1024 + g * P:i * 1024 + (g + 1) * P],
                                   WS[:, g, :], start=True, stop=True)
                mm.then_inc(K.sem("mixed"), 1)
    K.done(loaded=64, stats=8, moments=4, step_dve=12, step_act=2, mixed=8, taken_dve=8, followed=8, gated=8)
    linear_deep(K, 2, tiles_in(Y), 8, add_to(K.X))


def fourier(K, FD, YD, base):
    nc = K.nc
    DFT = K.big(base, 8 * T).rearrange("p (i n) -> p i n", i=TT)
    CS = K.big(base + 8 * T, 8 * T).rearrange("p (g n) -> p g n", g=4)
    DD = K.big(base + 16 * T, 2 * P)
    WF = K.big(base + 16 * T + 2 * P, 4 * P).rearrange("p (g n) -> p g n", g=4)
    WC = K.big(base + 16 * T + 6 * P, 8 * P).rearrange("p (g n) -> p g n", g=4)
    with nc.Block() as block:
        @block.sync
        def _(sp):
            sp.dma_start(DFT, K.ins["dft"]).then_inc(K.sem("loaded"), 16)
            sp.dma_start(DD, K.ins["dft_d"]).then_inc(K.sem("loaded"), 16)
            sp.dma_start(WF, K.ins["fnet_w"]).then_inc(K.sem("loaded"), 16)

        @block.tensor
        def _(pe):
            pe.wait_ge(K.sem("loaded"), K.count("loaded", 48))
            for h in range(2):
                mm = pe.matmul(K.ps[:, h, :], DD[:, h * P:(h + 1) * P], WF.rearrange("p g n -> p (g n)"), start=True,
                               stop=True)
            mm.then_inc(K.sem("product"), 1)
            for g in range(4):
                pe.wait_ge(K.sem("taken_act"), K.count("taken_act", g - 1))
                pe.wait_ge(K.sem("taken_dve"), K.count("taken_dve", g - 1))
                for h in range(2):
                    for i in range(TT):
                        mm = pe.matmul(K.ps[:, 2 + 2 * (g % 2) + h, :], FD[:, i * 512 + g * P:i * 512 + (g + 1) * P],
                                       DFT[:, i, h * T:(h + 1) * T], start=(i == 0), stop=(i == TT - 1))
                    mm.then_inc(K.sem("summed"), 1)
            pe.wait_ge(K.sem("step_dve"), K.count("step_dve", 2))
            for g in range(4):
                pe.wait_ge(K.sem("taken_act"), K.count("taken_act", g + 1))
                pe.wait_ge(K.sem("taken_dve"), K.count("taken_dve", g + 1))
                pe.wait_ge(K.sem("followed"), K.count("followed", g - 1))
                for h in range(2):
                    mm = pe.matmul(K.ps[:, 6 + g % 2, :], WC[:, g, h * P:(h + 1) * P], CS[:, g, h * T:(h + 1) * T],
                                   start=(h == 0), stop=(h == 1))
                mm.then_inc(K.sem("mixed"), 1)

        @block.vector
        def _(dve):
            dve.wait_ge(K.sem("product"), K.count("product", 1))
            for h in range(2):
                dve.tensor_copy(WC[:, :, h * P:(h + 1) * P], K.ps[:, h, :].rearrange("p (g n) -> p g n", g=4))\
                   .then_inc(K.sem("step_dve"), 1)
            for g in range(4):
                dve.wait_ge(K.sem("summed"), K.count("summed", 2 * g + 2))
                dve.tensor_copy(CS[:, g, T:], K.ps[:, 3 + 2 * (g % 2), :]).then_inc(K.sem("taken_dve"), 1)
            for g in range(4):
                dve.wait_ge(K.sem("mixed"), K.count("mixed", g + 1))
                s = slice(g * T, (g + 1) * T)
                dve.tensor_tensor(YD[:, s], K.ps[:, 6 + g % 2, :], YD[:, s], ALU.mult).then_inc(K.sem("followed"), 1)

        @block.scalar
        def _(act):
            for g in range(4):
                act.wait_ge(K.sem("summed"), K.count("summed", 2 * g + 1))
                act.activation(CS[:, g, 0:T], K.ps[:, 2 + 2 * (g % 2), :], ACT.Copy).then_inc(K.sem("taken_act"), 1)
    K.done(loaded=48, product=1, summed=8, taken_act=4, taken_dve=4, followed=4, step_dve=2, mixed=4)


class Marks:

    def __init__(self, K, name, steps):
        self.K, self.name, self.steps, self.at = K, name, steps.split(), 0
        self.sem = K.sem(name)

    def step(self, name):
        assert self.steps[self.at % len(self.steps)] == name, (self.steps[self.at % len(self.steps)], name)
        self.at += 1
        return self.sem

    def count(self, n, name):
        return self.K.count(self.name, len(self.steps) * n + self.steps.index(name) + 1)

    def done(self, rounds):
        self.K.done(**{self.name: len(self.steps) * rounds})


def wkv(K, base, WDA, W2, RZ, out):
    nc = K.nc
    at = base

    def room(n):
        nonlocal at
        at += n
        return K.big(at - n, n)
    units = lambda a: a.rearrange("p (n t) -> p n t", t=P)
    RAW = room(6 * T).rearrange("p (b m t) -> p b m t", b=2, m=3)
    ZG = room(2 * T).rearrange("p (b t) -> p b t", b=2)
    AR = room(4 * T).rearrange("p (d i m t) -> p d i m t", d=2, i=TT, m=2)
    BT, KT, VT, G = (room(2 * T).rearrange("p (d i t) -> p d i t", d=2, i=TT) for _ in range(4))
    MRB = room(2 * T).rearrange("p (d n t) -> p d n t", d=2, t=64)
    XTC = room(2 * T).rearrange("p (d n t) -> p d n t", d=2, t=64)
    YV = room(2 * T).rearrange("p (d t) -> p d t", d=2)
    BO = room(2 * T).rearrange("p (d t) -> p d t", d=2)
    YS = room(T)
    BK = room(2 * T).rearrange("p (m t) -> p m t", m=2)
    W2F = room(P)
    S, SE = room(P), room(P)
    GS, SAN = room(P), room(P)
    EE = room(16).rearrange("p (d n) -> p d n", d=2)
    R = [room(T) for _ in range(10)]
    RQ, KQ, VQ, LW, L, AA, EP, EN, RN, TMP = R
    pair = lambda n: K.big(at - (10 - n) * T, 2 * T)
    AS, X, XT, T1, C = (units(pair(n)) for n in (0, 2, 4, 6, 8))
    MAK, MRK = C, T1
    D2 = ("resets64_f", "resets64_b")
    i4 = lambda a: a.rearrange("p (i n) -> p i n", n=P)
    wide = lambda b: K.psflat[:, b * 512:b * 512 + 1024].rearrange("p (n t) -> p n t", t=P)
    first = K.tile
    mu = lambda d, m, c: K.v(f"mu{d}")[:, ds(8 * m + c, 1)]
    omm = lambda d, m, c: K.small[:, ds(25 * d + 8 * m + c, 1)]
    cv = lambda name, c: K.v(name)[:, ds(c, 1)]
    rate = float(np.exp(np.float32(-0.5)))

    PM = Marks(K, "wkv_pe", "wa kkn bon tv tb tk sa sk srb t0 g yv " +
               " ".join(f"t{l}a t{l}b ct{l}a ct{l}b" + (f" cx{l}a cx{l}b" if l < 5 else "") for l in range(1, 6)))
    AM = Marks(K, "wkv_act", "sw aa sqk ln rn ep en eplus ee vt bt kt as g yv " + " ".join(f"t{l}a t{l}b" for l in range(1, 6)) +
               " xtc0 xtc1")
    DM = Marks(K, "wkv_dve", "r k v lw scan lprev max kk ahat rhat b bhat a1 kp khat rk bo bo2 mak mrb0 mrb1 mrk " +
               "xt0 x0 " +
               " ".join(f"xt{l}a xt{l}b" + (f" x{l}a x{l}b" if l < 5 else "") for l in range(1, 6)))
    GM = Marks(K, "wkv_pool", "w2f pr pk pv " + " ".join(f"c{l}" for l in range(6)))

    units_of = lambda half: range(4) if half == "a" else range(4, 8)
    in_half = lambda a, half: a[:, 0:4, :] if half == "a" else a[:, 4:8, :]

    def chunk(d, j):
        m = j if d == 0 else 7 - j
        return m // 2, m % 2

    def rounds(eng, step, finish):
        step(0, 0, 0, 0, None, None, 0)
        step(1, 1, 0, 0, 0, 0, 0)
        with eng.Fori(0, 3) as r:
            for o in range(2):
                c = 2 * r + 1 + o
                par = (1 + o) % 2
                step(4 * r + 2 + 2 * o, 0, c, par, 4 * r + 1 + 2 * o, 1, r + 1)
                step(4 * r + 3 + 2 * o, 1, c, par, 4 * r + 2 + 2 * o, 0, r + 1, (2 * r + o, 1 - par))
        step(14, 0, 7, 1, 13, 1, None)
        step(15, 1, 7, 1, 14, 0, None, (6, 0))
        step(None, None, 8, None, 15, 1, None)
        for part in range(2):
            finish(part, 7, 1)

    with nc.Block() as block:
        @block.sync
        def _(sp):
            def one(c, r, slot):
                sp.wait_ge(K.sem("projected"), K.count("projected", 4 * (c + 1)))
                sp.dma_start(K.W[:, slot, :], K.wstream[ds(first + 2 + c, 1), :, :].rearrange("g p n -> p (g n)"))\
                  .then_inc(K.landed[slot], 16)
            with sp.Fori(0, 4) as r:
                one(2 * r, r, first % 2)
                one(2 * r + 1, r, (first + 1) % 2)

        @block.gpsimd
        def _(pool):
            def step(n, d, c, par, p, pd, nth, fin=None):
                if n is not None:
                    pool.wait_ge(PM.sem, PM.count(n - 1, "wa"))
                    pool.tensor_copy(W2F, W2[:, ds(d * 1024 + c * P, P)]).then_inc(GM.step("w2f"), 1)
                    pool.wait_ge(K.sem("raw_kept"), K.count("raw_kept", 4 * c + 3))
                    pool.wait_ge(DM.sem, DM.count(n - 1, "xt5b"))
                    for m, (x, name) in enumerate(((RQ, "pr"), (KQ, "pk"), (VQ, "pv"))):
                        pool.tensor_tensor(x, RAW[:, par, m, :], omm(d, m, c).broadcast_to([P, T]), ALU.mult).then_inc(GM.step(name), 1)
                if p is not None:
                    pool.wait_ge(K.sem("ch_s"), K.count("ch_s", 8 * p))
                    pool.wait_ge(K.sem("ch_ys"), K.count("ch_ys", 8 * p))
                    K.apart(pool)
                    pool.memset(S, 0.0).then_inc(K.sem("s_zero"), 1)
                    pool.wait_ge(K.sem("s_zero"), K.count("s_zero", p + 1))

                def scale(j):
                    if p is None:
                        return
                    i, b = chunk(pd, j)
                    pool.wait_ge(K.sem("ch_s"), K.count("ch_s", 8 * p + j))
                    e = EE[:, pd, 2 * i + b:2 * i + b + 1]
                    pool.wait_ge(AM.sem, AM.count(p, "ee"))
                    K.apart(pool)
                    pool.tensor_scalar(SE, S, e, None, ALU.mult).then_inc(K.sem("ch_t"), 1)
                scale(0)
                scale(1)
                for l in range(6):
                    if n is not None:
                        pool.wait_ge(AM.sem, AM.count(n, "as"))
                        if l:
                            pool.wait_ge(PM.sem, PM.count(n, f"t{l - 1}b" if l > 1 else "g"))
                        mask = K.c(f"{'low' if d == 0 else 'up'}{l}").unsqueeze(1).broadcast_to([P, 8, P])
                        pool.tensor_tensor(C if l else X, AS, mask, ALU.mult).then_inc(GM.step(f"c{l}"), 1)
                    scale(l + 2)
            rounds(pool, step, lambda part, c, par: None)

        @block.tensor
        def _(pe):
            ident, same = K.c("ident"), K.c("same64")

            def project(par, m):
                slot = (first + par) % 2
                w = K.W[:, slot, :].rearrange("p (k n) -> p k n", k=8)
                for k in range(8):
                    mm = pe.matmul(K.ps[:, 2 + m % 2, :], w[:, k, m * P:(m + 1) * P], K.H[:, k, :], start=(k == 0),
                                   stop=(k == 7))
                mm.then_inc(K.sem("projected"), 1)

            def ch_g(p, pd, j):
                if p is None:
                    return
                i, b = chunk(pd, j)
                t = slice(64 * b, 64 * b + 64)
                if j == 0:
                    pe.wait_ge(AM.sem, AM.count(p, "xtc1"))
                pe.wait_ge(K.sem("s_zero"), K.count("s_zero", p + 1))
                pe.wait_ge(K.sem("ch_s"), K.count("ch_s", 8 * p + j))
                pe.matmul(K.ps[t, 6, 0:P], AR[:, pd, i, 0, t], S, start=True, stop=True, skip_group_check=True)\
                  .then_inc(K.sem("ch_g"), 1)
                if j == 0:
                    pe.wait_ge(K.sem("y_sum"), K.count("y_sum", p))
                pe.matmul(K.ps[:, 7, i * P + 64 * b:i * P + 64 * b + 64], S, AR[:, pd, i, 1, t], start=True, stop=False,
                          skip_group_check=True)

            def ch_sa(p, pd, j):
                if p is None:
                    return
                i, b = chunk(pd, j)
                t = slice(64 * b, 64 * b + 64)
                pe.wait_ge(K.sem("ch_gk"), K.count("ch_gk", 8 * p + j + 1))
                K.apart(pe)
                for h in range(2):
                    mm = pe.matmul(K.ps[t, 6, P + 64 * h:P + 64 * h + 64], XTC[t, pd, 4 * h + i, :],
                                   GS[t, 64 * h:64 * h + 64], start=True, stop=True, skip_group_check=True)
                mm.then_inc(K.sem("ch_sa"), 1)

            def ch_ys(p, pd, j):
                if p is None:
                    return
                i, b = chunk(pd, j)
                t = slice(64 * b, 64 * b + 64)
                cols = slice(i * P + 64 * b, i * P + 64 * b + 64)
                pe.wait_ge(K.sem("ch_san"), K.count("ch_san", 8 * p + j + 1))
                K.apart(pe)
                for h in range(2):
                    r = slice(64 * h, 64 * h + 64)
                    pe.matmul(K.ps[r, 7, cols], SAN[t, 64 * h:64 * h + 64], MRB[t, pd, 4 * h + i, :], start=False,
                              stop=True, skip_group_check=True)
                pe.matmul(K.ps[:, 6, 256:384], BT[t, pd, i, :], SAN[t, :], start=True, stop=False,
                          skip_group_check=True)
                pe.matmul(K.ps[:, 6, 256:384], KT[t, pd, i, :], VT[t, pd, i, :], start=False, stop=True,
                          skip_group_check=True).then_inc(K.sem("ch_ys"), 1)

            def finish(part, c, par):
                if part == 0:
                    pe.wait_ge(K.sem("y_sum"), K.count("y_sum", 2 * c + 2))
                    pe.matmul(K.ps[:, 5, :], same, YS, start=True, stop=True).then_inc(K.sem("fin_pe"), 1)
                else:
                    pe.wait_ge(K.sem("fin_act"), K.count("fin_act", 3 * c + 1))
                    pe.matmul(K.ps[:, 5, :], same, K.sq[:, 1, :], start=True, stop=True).then_inc(K.sem("fin_pe"), 1)

            def step(n, d, c, par, p, pd, nth, fin=None):
                def projection(half):
                    if nth is None:
                        return
                    q = 1 - par
                    if d == 0 and half == 0:
                        pe.wait_ge(K.landed[(first + q) % 2], 16 * ((first + q) // 2 + 1) + 16 * nth)
                    m = 2 * d + half
                    pe.wait_ge(K.sem("raw_kept"), K.count("raw_kept", 4 * (c + 1) + m - 1))
                    pe.wait_ge(DM.sem, DM.count(n - 1, "mrk"))
                    project(q, m)
                if n is not None:
                    pe.wait_ge(GM.sem, GM.count(n, "w2f"))
                    pe.wait_ge(DM.sem, DM.count(n - 1, "xt5b"))
                    pe.matmul(K.ps[:, 0, :], W2F[0:64, :], WDA[0:64, d * T:(d + 1) * T], start=True, stop=True)
                    pe.matmul(K.ps[:, 1, :], W2F[64:128, :], WDA[64:128, d * T:(d + 1) * T], start=True,
                                     stop=True).then_inc(PM.step("wa"), 1)
                ch_g(p, pd, 0)
                if fin is not None:
                    pe.wait_ge(DM.sem, DM.count(n - 1, "xt5b"))
                    finish(0, *fin)
                if n is not None:
                    projection(0)
                ch_sa(p, pd, 0)
                if n is not None:
                    pe.wait_ge(AM.sem, AM.count(n, "sqk"))
                    pe.wait_ge(DM.sem, DM.count(n - 1, "xt5b"))
                    pe.matmul(K.ps[:, 4, :], same, K.sq[:, 0, :], start=True, stop=True).then_inc(PM.step("kkn"), 1)
                if fin is not None:
                    finish(1, *fin)
                ch_ys(p, pd, 0)
                ch_g(p, pd, 1)
                if n is not None:
                    projection(1)
                if n is not None:
                    pe.wait_ge(DM.sem, DM.count(n, "rk"))
                    if fin is not None:
                        pe.wait_ge(K.sem("fin_act"), K.count("fin_act", 3 * fin[0] + 2))
                    pe.matmul(K.ps[:, 5, :], same, RQ, start=True, stop=True).then_inc(PM.step("bon"), 1)
                ch_sa(p, pd, 1)
                if n is not None:
                    for i in range(TT):
                        mm = pe.transpose(K.ps[:, 4, i * P:(i + 1) * P], VQ[:, i * P:(i + 1) * P], ident)
                    mm.then_inc(PM.step("tv"), 1)
                ch_ys(p, pd, 1)
                if n is not None:
                    pe.wait_ge(DM.sem, DM.count(n, "bo2"))
                    for i in range(TT):
                        mm = pe.transpose(K.ps[:, 5, i * P:(i + 1) * P], BK[:, 0, i * P:(i + 1) * P], ident)
                    mm.then_inc(PM.step("tb"), 1)
                    pe.wait_ge(AM.sem, AM.count(n, "vt"))
                    for i in range(TT):
                        mm = pe.transpose(K.ps[:, 4, i * P:(i + 1) * P], BK[:, 1, i * P:(i + 1) * P], ident)
                    mm.then_inc(PM.step("tk"), 1)
                    un = [(i, h) for h in range(2) for i in range(TT)]
                    pe.wait_ge(AM.sem, AM.count(n, "aa"))
                    tile = lambda i: slice(i * P, (i + 1) * P)
                    hr = lambda h: slice(64 * h, 64 * h + 64)
                    for u, (i, h) in enumerate(un):
                        mm = pe.matmul(K.psflat[:, u * P:(u + 1) * P], AR[hr(h), d, i, 0, :], BK[hr(h), 0, tile(i)],
                                       start=True, stop=True)
                    mm.then_inc(PM.step("sa"), 1)
                    pe.wait_ge(AM.sem, AM.count(n, "kt"))
                    if nth is not None:
                        pe.wait_ge(K.sem("raw_kept"), K.count("raw_kept", 4 * (c + 1) + 2 * d + 2))
                    for u, (i, h) in enumerate(un):
                        o = 1024 + u * 256
                        mm = pe.matmul(K.psflat[:, o:o + 256], BK[hr(h), 1, tile(i)],
                                       AR[hr(h), d, i, :, :].rearrange("p m t -> p (m t)"), start=True, stop=True)
                    mm.then_inc(PM.step("sk"), 1)
                    pe.wait_ge(AM.sem, AM.count(n, "as"))
                    for u, (i, h) in enumerate(un):
                        mm = pe.matmul(K.psflat[:, u * P:(u + 1) * P], BK[hr(h), 0, tile(i)], AR[hr(h), d, i, 1, :],
                                       start=True, stop=True)
                    mm.then_inc(PM.step("srb"), 1)
                    pe.wait_ge(DM.sem, DM.count(n, "mrb1"))
                    pe.wait_ge(GM.sem, GM.count(n, "c0"))
                    for u in range(8):
                        mm = pe.transpose(wide(0)[:, u, :], X[:, u, :], ident)
                    mm.then_inc(PM.step("t0"), 1)
                    pe.wait_ge(DM.sem, DM.count(n, "mrk"))
                    for u, (i, h) in enumerate(un):
                        mm = pe.matmul(K.ps[:, 2, i * P + 64 * h:i * P + 64 * h + 64], MAK[:, u, :], VT[:, d, i, hr(h)], start=True,
                                       stop=True)
                    mm.then_inc(PM.step("g"), 1)
                    for u, (i, h) in enumerate(un):
                        mm = pe.matmul(K.ps[hr(h), 3, tile(i)], VT[:, d, i, hr(h)], MRK[:, u, :], start=True,
                                       stop=True, skip_group_check=True)
                    mm.then_inc(PM.step("yv"), 1)
                for l in range(6):
                    if n is not None and l:
                        pe.wait_ge(GM.sem, GM.count(n, f"c{l}"))
                        for half in "ab":
                            pe.wait_ge(DM.sem, DM.count(n, f"xt{l - 1}{half}" if l > 1 else "xt0"))
                            for u in units_of(half):
                                mm = pe.matmul(wide(0)[:, u, :], C[:, u, :], XT[:, u, :], start=True, stop=True)
                            mm.then_inc(PM.step(f"t{l}{half}"), 1)
                    ch_g(p, pd, l + 2)
                    if n is not None and l:
                        pe.wait_ge(DM.sem, DM.count(n, f"x{l - 1}b" if l > 1 else "x0"))
                        for half in "ab":
                            pe.wait_ge(AM.sem, AM.count(n, f"t{l}{half}"))
                            for u in units_of(half):
                                mm = pe.matmul(wide(4)[:, u, :], X[:, u, :], T1[:, u, :], start=True, stop=True)
                            mm.then_inc(PM.step(f"ct{l}{half}"), 1)
                    ch_sa(p, pd, l + 2)
                    if n is not None and 0 < l < 5:
                        for half in "ab":
                            for u in units_of(half):
                                mm = pe.matmul(wide(2)[:, u, :], T1[:, u, :], X[:, u, :], start=True, stop=True)
                            mm.then_inc(PM.step(f"cx{l}{half}"), 1)
                    ch_ys(p, pd, l + 2)

            pe.wait_ge(K.landed[first % 2], 16 * (first // 2 + 1))
            for m in range(4):
                pe.wait_ge(K.sem("raw_kept"), K.count("raw_kept", m - 1))
                project(0, m)
            rounds(pe, step, finish)

        @block.scalar
        def _(act):
            def keep(c, par, m):
                act.wait_ge(K.sem("projected"), K.count("projected", 4 * c + m + 1))
                if m < 3:
                    ins = act.activation(RAW[:, par, m, :], K.ps[:, 2 + m % 2, :], ACT.Copy)
                else:
                    ins = act.activation(ZG[:, par, :], K.ps[:, 3, :], ACT.Silu)
                ins.then_inc(K.sem("raw_kept"), 1)

            def san(p, pd, j):
                if p is None:
                    return
                i, b = chunk(pd, j)
                t = slice(64 * b, 64 * b + 64)
                act.wait_ge(K.sem("ch_sa"), K.count("ch_sa", 8 * p + j + 1))
                act.wait_ge(K.sem("ch_ys"), K.count("ch_ys", 8 * p + j))
                act.activation(SAN[t, :], K.ps[t, 6, P:2 * P], ACT.Copy, scale=-1.0).then_inc(K.sem("ch_san"), 1)

            def finish(part, c, par):
                if part == 0:
                    act.wait_ge(K.sem("fin_dve"), K.count("fin_dve", 4 * c + 1))
                    act.activation(K.sq[:, 1, :], YS, ACT.Square).then_inc(K.sem("fin_act"), 1)
                else:
                    act.wait_ge(K.sem("fin_pe"), K.count("fin_pe", 2 * c + 2))
                    act.activation(K.ln[:, :], K.ps[:, 5, :], ACT.Ln, scale=1.0 / 64, bias=K.c("eps_gn"))\
                       .then_inc(K.sem("fin_act"), 1)
                    act.wait_ge(K.sem("fin_act"), K.count("fin_act", 3 * c + 2))
                    act.activation(K.rstd[:, :], K.ln[:, :], ACT.Exp, scale=-0.5).then_inc(K.sem("fin_act"), 1)

            def step(n, d, c, par, p, pd, nth, fin=None):
                if n is not None:
                    act.wait_ge(PM.sem, PM.count(n, "wa"))
                    act.wait_ge(DM.sem, DM.count(n - 1, "xt5b"))
                    act.wait_ge(AM.sem, AM.count(n - 1, "xtc1"))
                    act.activation(LW, K.ps[:, 0, :], ACT.Sigmoid, bias=cv(f"w0_{d}", c)).then_inc(AM.step("sw"), 1)
                    act.activation(AA, K.ps[:, 1, :], ACT.Sigmoid, bias=cv(f"a0_{d}", c)).then_inc(AM.step("aa"), 1)
                    act.wait_ge(DM.sem, DM.count(n, "k"))
                    act.wait_ge(PM.sem, PM.count(n - 1, "kkn"))
                    K.apart(act)
                    act.activation(K.sq[:, 0, :], KQ, ACT.Square, scale=cv("k_k", c)).then_inc(AM.step("sqk"), 1)
                if fin is not None:
                    finish(0, *fin)
                san(p, pd, 0)
                if n is not None:
                    if nth is not None:
                        if d == 0:
                            act.wait_ge(DM.sem, DM.count(n - 1, "v"))
                        keep(c + 1, 1 - par, 2 * d)
                    if fin is not None:
                        finish(1, *fin)
                    act.wait_ge(DM.sem, DM.count(n, "max"))
                    act.activation(RN, RN, ACT.Ln).then_inc(AM.step("ln"), 1)
                    act.wait_ge(AM.sem, AM.count(n, "ln"))
                    act.activation(RN, RN, ACT.Exp, scale=-0.5).then_inc(AM.step("rn"), 1)
                    act.activation(EP, EP, ACT.Exp).then_inc(AM.step("ep"), 1)
                    act.activation(EN, L, ACT.Exp, scale=-1.0).then_inc(AM.step("en"), 1)
                    act.wait_ge(AM.sem, AM.count(n, "en"))
                    act.activation(L, L, ACT.Exp).then_inc(AM.step("eplus"), 1)
                    act.wait_ge(AM.sem, AM.count(n, "eplus"))
                    act.wait_ge(K.sem("ch_s"), K.count("ch_s", 8 * n - 8))
                    end = slice(63, 64) if d == 0 else slice(0, 1)
                    act.activation(EE[:, d, :], L.rearrange("p (n t) -> p n t", t=64)[:, :, end]
                                          .rearrange("p n o -> p (n o)"), ACT.Copy).then_inc(AM.step("ee"), 1)
                    if nth is not None:
                        if d == 1:
                            act.wait_ge(K.sem("fin_dve"), K.count("fin_dve", 4 * c))
                        keep(c + 1, 1 - par, 2 * d + 1)
                san(p, pd, 1)
                if n is not None:
                    for name, src, dst, bank in (("vt", "tv", VT, 4), ("bt", "tb", BT, 5), ("kt", "tk", KT, 4)):
                        act.wait_ge(PM.sem, PM.count(n, src))
                        act.activation(dst[:, d].rearrange("p i t -> p (i t)"), K.ps[:, bank, :], ACT.Copy).then_inc(AM.step(name), 1)
                    act.wait_ge(PM.sem, PM.count(n, "sa"))
                    act.activation(AS, wide(0), ACT.Copy).then_inc(AM.step("as"), 1)
                    act.wait_ge(PM.sem, PM.count(n, "g"))
                    act.activation(G[:, d].rearrange("p i t -> p (i t)"), K.ps[:, 2, :], ACT.Copy).then_inc(AM.step("g"), 1)
                    act.wait_ge(PM.sem, PM.count(n, "yv"))
                    act.activation(YV[:, d, :], K.ps[:, 3, :], ACT.Copy).then_inc(AM.step("yv"), 1)
                for l in range(6):
                    if n is not None and l:
                        for half in "ab":
                            act.wait_ge(PM.sem, PM.count(n, f"t{l}{half}"))
                            act.activation(in_half(T1, half), in_half(wide(0), half), ACT.Copy)\
                               .then_inc(AM.step(f"t{l}{half}"), 1)
                    san(p, pd, l + 2)
                if n is not None:
                    act.wait_ge(DM.sem, DM.count(n, "xt5b"))
                    for b in range(2):
                        t = slice(64 * b, 64 * b + 64)
                        act.activation(XTC[t, d, :, :], XT[t, :, t], ACT.Copy).then_inc(AM.step(f"xtc{b}"), 1)

            for m in range(4):
                keep(0, 0, m)
            rounds(act, step, finish)

        @block.vector
        def _(dve):
            def gk(p, pd, j):
                if p is None:
                    return
                i, b = chunk(pd, j)
                t = slice(64 * b, 64 * b + 64)
                if j == 0:
                    dve.wait_ge(AM.sem, AM.count(p, "g"))
                dve.wait_ge(K.sem("ch_g"), K.count("ch_g", 8 * p + j + 1))
                dve.wait_ge(K.sem("ch_sa"), K.count("ch_sa", 8 * p + j))
                dve.tensor_tensor(GS[t, :], K.ps[t, 6, 0:P], G[t, pd, i, :], ALU.add).then_inc(K.sem("ch_gk"), 1)

            def upd(p, pd, j):
                if p is None:
                    return
                i, b = chunk(pd, j)
                dve.wait_ge(K.sem("ch_ys"), K.count("ch_ys", 8 * p + j + 1))
                dve.wait_ge(K.sem("ch_t"), K.count("ch_t", 8 * p + j + 1))
                for h in range(2):
                    r = slice(64 * h, 64 * h + 64)
                    ins = dve.scalar_tensor_tensor(S[r, r], K.ps[r, 6, 256 + 64 * h:320 + 64 * h],
                                                   EE[r, pd, 2 * i + b:2 * i + b + 1], SE[r, r], ALU.mult, ALU.add)
                ins.then_inc(K.sem("ch_s"), 1)

            def finish(part, c, par):
                if part == 0:
                    dve.wait_ge(K.sem("fin_pe"), K.count("fin_pe", 2 * c + 1))
                    dve.scalar_tensor_tensor(YS, K.ps[:, 5, :], -1.0 / 64, YS, ALU.mult, ALU.add)\
                       .then_inc(K.sem("fin_dve"), 1)
                else:
                    dve.wait_ge(K.sem("fin_act"), K.count("fin_act", 3 * c + 3))
                    dve.scalar_tensor_tensor(YS, YS, cv("lnx_g", c), K.rstd[:, :], ALU.mult, ALU.mult)\
                       .then_inc(K.sem("fin_dve"), 1)
                    dve.wait_ge(K.sem("fin_dve"), K.count("fin_dve", 4 * c + 2))
                    dve.scalar_tensor_tensor(YS, YS, cv("lnx_b", c), BO[:, par, :], ALU.add, ALU.add)\
                       .then_inc(K.sem("fin_dve"), 1)
                    dve.wait_ge(K.sem("fin_dve"), K.count("fin_dve", 4 * c + 3))
                    dve.tensor_tensor(out[:, ds(c * T, T)], YS, ZG[:, par, :], ALU.mult)\
                       .then_inc(K.sem("fin_dve"), 1)

            def step(n, d, c, par, p, pd, nth, fin=None):
                gk(p, pd, 0)
                if n is not None:
                    lo, hi = slice(0, T - 1), slice(1, T)
                    dst, src = (hi, lo) if d == 0 else (lo, hi)
                    for m, (x, name, pn) in enumerate(((RQ, "r", "pr"), (KQ, "k", "pk"), (VQ, "v", "pv"))):
                        dve.wait_ge(GM.sem, GM.count(n, pn))
                        dve.scalar_tensor_tensor(x[:, dst], RAW[:, par, m, src], mu(d, m, c), x[:, dst],
                                                        ALU.mult, ALU.add).then_inc(DM.step(name), 1)
                if fin is not None:
                    finish(0, *fin)
                if n is not None:
                    dve.wait_ge(AM.sem, AM.count(n, "sw"))
                    dve.tensor_scalar(LW, LW, -rate, None, ALU.mult).then_inc(DM.step("lw"), 1)
                    dve.wait_ge(DM.sem, DM.count(n, "lw"))
                    dve.wait_ge(AM.sem, AM.count(n - 1, "xtc1"))
                    f = (lambda a: a) if d == 0 else (lambda a: a[:, ::-1])
                    dve.tensor_tensor_scan(f(L), f(RZ[:, d * T:(d + 1) * T]), f(LW), 0.0, ALU.mult, ALU.add).then_inc(DM.step("scan"), 1)
                    dve.wait_ge(DM.sem, DM.count(n, "scan"))
                    dve.tensor_tensor(EP, L, LW, ALU.subtract).then_inc(DM.step("lprev"), 1)
                    dve.wait_ge(PM.sem, PM.count(n, "kkn"))
                    dve.tensor_scalar(RN, K.ps[:, 4, :], 1e-12, None, ALU.max).then_inc(DM.step("max"), 1)
                upd(p, pd, 0)
                gk(p, pd, 1)
                if n is not None:
                    if fin is not None:
                        finish(1, *fin)
                    dve.wait_ge(AM.sem, AM.count(n, "rn"))
                    dve.scalar_tensor_tensor(RN, KQ, cv("k_k", c), RN, ALU.mult, ALU.mult).then_inc(DM.step("kk"), 1)
                    dve.wait_ge(AM.sem, AM.count(n, "ee"))
                    dve.wait_ge(DM.sem, DM.count(n, "kk"))
                    dve.tensor_tensor(AR[:, d, :, 0, :], i4(RN), i4(EP), ALU.mult).then_inc(DM.step("ahat"), 1)
                    dve.tensor_tensor(AR[:, d, :, 1, :], i4(RQ), i4(L), ALU.mult).then_inc(DM.step("rhat"), 1)
                    dve.tensor_tensor(LW, RN, AA, ALU.mult).then_inc(DM.step("b"), 1)
                    dve.wait_ge(DM.sem, DM.count(n, "b"))
                    dve.tensor_tensor(BK[:, 0, :], LW, EN, ALU.mult).then_inc(DM.step("bhat"), 1)
                    dve.tensor_scalar(AA, AA, 1.0, cv("k_a", c), ALU.subtract, ALU.mult).then_inc(DM.step("a1"), 1)
                    dve.wait_ge(DM.sem, DM.count(n, "a1"))
                    dve.scalar_tensor_tensor(KQ, AA, 1.0, KQ, ALU.add, ALU.mult).then_inc(DM.step("kp"), 1)
                    dve.wait_ge(DM.sem, DM.count(n, "kp"))
                    dve.tensor_tensor(BK[:, 1, :], KQ, EN, ALU.mult).then_inc(DM.step("khat"), 1)
                    dve.scalar_tensor_tensor(RQ, RQ, cv("r_k", c), KQ, ALU.mult, ALU.mult).then_inc(DM.step("rk"), 1)
                    dve.wait_ge(PM.sem, PM.count(n, "bon"))
                    if d == 0:
                        dve.tensor_tensor(BO[:, par, :], K.ps[:, 5, :], VQ, ALU.mult).then_inc(DM.step("bo"), 1)
                        dve.tensor_copy(TMP[:, 0:64], VQ[:, 0:64]).then_inc(DM.step("bo2"), 1)
                    else:
                        dve.tensor_tensor(TMP, K.ps[:, 5, :], VQ, ALU.mult).then_inc(DM.step("bo"), 1)
                        dve.wait_ge(DM.sem, DM.count(n, "bo"))
                        dve.tensor_tensor(BO[:, par, :], BO[:, par, :], TMP, ALU.add).then_inc(DM.step("bo2"), 1)
                upd(p, pd, 1)
                if n is not None:
                    strict, incl = (K.c(x) for x in (("lt64", "le64") if d == 0 else ("gt64", "ge64")))
                    dve.wait_ge(PM.sem, PM.count(n, "sk"))
                    dve.wait_ge(DM.sem, DM.count(n, "bo2"))
                    sk = K.psflat[:, 1024:3072].rearrange("p (n m t) -> p n m t", m=2, t=P)
                    dve.tensor_tensor(MAK, sk[:, :, 0, :], strict.unsqueeze(1).broadcast_to([P, 8, P]), ALU.mult).then_inc(DM.step("mak"), 1)
                    dve.wait_ge(PM.sem, PM.count(n, "srb"))
                    for b in range(2):
                        t = slice(64 * b, 64 * b + 64)
                        dve.tensor_tensor(MRB[t, d, :, :], wide(0)[t, :, t],
                                                 incl[t, t].unsqueeze(1).broadcast_to([64, 8, 64]), ALU.mult).then_inc(DM.step(f"mrb{b}"), 1)
                    dve.tensor_tensor(MRK, sk[:, :, 1, :], incl.unsqueeze(1).broadcast_to([P, 8, P]), ALU.mult).then_inc(DM.step("mrk"), 1)
                for l in range(6):
                    gk(p, pd, l + 2)
                    if n is not None and l == 0:
                        ones = K.c("ident").unsqueeze(1).broadcast_to([P, 8, P])
                        dve.wait_ge(PM.sem, PM.count(n, "t0"))
                        dve.tensor_tensor(XT, ones, wide(0), ALU.subtract).then_inc(DM.step("xt0"), 1)
                        dve.tensor_tensor(X, ones, X, ALU.subtract).then_inc(DM.step("x0"), 1)
                    if n is not None and l:
                        last = f"x{l - 1}b" if l > 1 else "x0"
                        dve.wait_ge(DM.sem, DM.count(n, last))
                        for half in "ab":
                            dve.wait_ge(PM.sem, PM.count(n, f"ct{l}{half}"))
                            x = in_half(XT, half)
                            dve.tensor_tensor(x, x, in_half(wide(4), half), ALU.subtract)\
                               .then_inc(DM.step(f"xt{l}{half}"), 1)
                        for half in "ab" if l < 5 else "":
                            dve.wait_ge(PM.sem, PM.count(n, f"cx{l}{half}"))
                            x = in_half(X, half)
                            dve.tensor_tensor(x, x, in_half(wide(2), half), ALU.subtract)\
                               .then_inc(DM.step(f"x{l}{half}"), 1)
                    upd(p, pd, l + 2)
                if p is not None:
                    dve.wait_ge(K.sem("ch_ys"), K.count("ch_ys", 8 * p + 8))
                    dve.wait_ge(AM.sem, AM.count(p, "yv"))
                    if pd == 0:
                        dve.tensor_tensor(YS, K.ps[:, 7, :], YV[:, pd, :], ALU.add).then_inc(K.sem("y_sum"), 1)
                    else:
                        dve.wait_ge(K.sem("y_sum"), K.count("y_sum", p))
                        dve.tensor_tensor(YS, YS, YV[:, pd, :], ALU.add).then_inc(K.sem("y_part"), 1)
                        dve.wait_ge(K.sem("y_part"), K.count("y_part", c))
                        dve.tensor_tensor(YS, YS, K.ps[:, 7, :], ALU.add).then_inc(K.sem("y_sum"), 1)

            rounds(dve, step, finish)
    for m in (PM, AM, DM, GM):
        m.done(16)
    K.done(projected=32, raw_kept=32, s_zero=16, ch_g=128, ch_gk=128, ch_sa=128, ch_san=128, ch_ys=128, ch_t=128,
           ch_s=128, y_sum=16, y_part=8, fin_pe=16, fin_act=24, fin_dve=32)
    K.tile += 8


def rwkv_layer(K):
    nc = K.nc
    YD = K.big(0, 4 * T)
    linear(K, 1, K.H, copy_to(YD, ACT.Silu), sides=("act",) * 4)
    FD = K.big(4 * T, 4 * T)
    linear(K, 1, K.H, tokens_to(FD, 512), token_major=True)
    fourier(K, FD, YD, 8 * T)
    WD = K.big(4 * T, T)
    linear(K, 1, K.H, copy_to(WD), banks=1)
    WDA, W2, RZ = K.big(5 * T, 2 * T), K.big(7 * T, 4 * T), K.big(11 * T, 2 * T)
    omm = K.small[:, 0:50]
    with nc.Block() as block:
        @block.sync
        def _(sp):
            sp.dma_start(K.x_kept, K.X.rearrange("p k t -> p (k t)")).then_inc(K.sem("loaded"), 16)
            sp.dma_start(W2, K.ins["w2a2"]).then_inc(K.sem("loaded"), 16)
            sp.dma_start(RZ, K.ins["resets64"]).then_inc(K.sem("loaded"), 16)
            sp.wait_ge(K.sem("loaded"), K.count("loaded", 48))

        @block.vector
        def _(dve):
            for d in range(2):
                dve.tensor_scalar(omm[:, 25 * d:25 * d + 25], K.v(f"mu{d}"), -1.0, 1.0, ALU.mult, ALU.add)\
                   .then_inc(K.sem("step_dve"), 1)
            for d in range(2):
                x = WDA[:, d * T:(d + 1) * T]
                lo, hi = slice(0, T - 1), slice(1, T)
                dst, src = (hi, lo) if d == 0 else (lo, hi)
                dve.wait_ge(K.sem("step_dve"), K.count("step_dve", 2 + 2 * d))
                dve.tensor_scalar(x, WD, omm[:, 25 * d + 24:25 * d + 25], None, ALU.mult).then_inc(K.sem("step_dve"), 1)
                dve.wait_ge(K.sem("step_dve"), K.count("step_dve", 3 + 2 * d))
                dve.scalar_tensor_tensor(x[:, dst], WD[:, src], K.v(f"mu{d}")[:, 24:25], x[:, dst], ALU.mult, ALU.add)\
                   .then_inc(K.sem("step_dve"), 1)

        @block.scalar
        def _(act):
            act.wait_ge(K.sem("step_dve"), K.count("step_dve", 6))
            act.activation(WDA[0:64, :], WDA[0:64, :], ACT.Tanh)
    K.done(loaded=48, step_dve=6)
    Y = K.X.rearrange("p k t -> p (k t)")
    wkv(K, 13 * T, WDA, W2, RZ, Y)
    K.X, K.H = K.H, K.X
    with nc.Block() as block:
        @block.sync
        def _(sp):
            sp.dma_start(K.X.rearrange("p k t -> p (k t)"), K.x_kept).then_inc(K.sem("loaded"), 16)
            sp.wait_ge(K.sem("loaded"), K.count("loaded", 16))
    K.done(loaded=16)
    linear_deep(K, 2, lambda k: K.H[:, k, :] if k < 8 else YD[:, (k - 8) * T:(k - 7) * T], 6, add_to(K.X))


SIGNALS = """square summed logged rstd scaled product taken_act taken_dve followed tile_used gated loaded
step_act step_dve step_pe step_pool q_fixed k_fixed v_fixed scores peak probs inverse weights turned turned_kept mixed
head_out first_map second_map
tap state tokens_major g_fixed row_sums normed between half_turned half_kept correction inverse_kept solved solved_kept
recalled v_new o_ready learnt d_ready d_pos decay row_decay a_beta a_ready masked qk_ready q_decayed
state_decayed rotated
evac_act evac_dve k_decayed states ctx_turned diag_ready sc_kept levels_ready kct_kept ctx_state kt_kept o_taken s0_kept
args dk_exp exp_levels exp_rest softplus logsig chain
centered glu tapped silu short taken_gate stats moments
wkv_pe wkv_act wkv_dve wkv_pool projected raw_kept s_zero ch_g ch_gk ch_sa ch_san ch_ys ch_t ch_s y_sum y_part
fin_pe fin_act fin_dve""".split()


def build(nc, ins, out, stages, ntiles, dump=None):
    with ExitStack() as ctx:
        K = Core(nc, ctx)
        K.ins = ins
        K.wstream, K.ntiles = ins["weights"], ntiles
        K.X = K.sb("x", [P, KD, T])
        K.H = K.sb("h", [P, KD, T])
        K.W = K.sb("w", [P, 2, TILE])
        K.const = K.sb("const", [P, NCONST])
        K.vecs = K.sb("vecs", [P, NVEC])
        K.small = K.sb("small", [P, 216])
        K.sq = K.sb("sq", [P, 2, T])
        K.ln = K.sb("ln", [P, T])
        K.rstd = K.sb("rstd", [P, T])
        K.bigbuf = K.sb("big", [P, NBIG])
        K.psflat = ctx.enter_context(nc.psum_tensor("ps", [P, 8 * 512], F32))
        K.ps = K.psflat.rearrange("p (b n) -> p b n", b=8)
        K.landed = [ctx.enter_context(nc.semaphore(f"weights_landed{s}")) for s in range(2)]
        K.landed_v = [ctx.enter_context(nc.semaphore(f"values_landed{s}")) for s in range(2)]
        K.x_kept = nc.dram_tensor("x_kept", [P, KD * T], F32, kind="Internal").ap()
        K.mod = K.small[:, 168:216]
        K.carried = ctx.enter_context(nc.semaphore("carried"))
        stored = ctx.enter_context(nc.semaphore("stored"))
        with nc.Block() as block:
            @block.sync
            def _(sp):
                for name in SIGNALS:
                    sp.sem_inc(K.declare(name), CREDIT)
                for s in range(2):
                    sp.dma_start(K.W[:, s, :], K.wstream[s, :, :]).then_inc(K.landed[s], 16)
                sp.dma_start(K.X[:, :, :], ins["xT"]).then_inc(stored, 16)
                sp.dma_start(K.const[:, :], ins["const"]).then_inc(stored, 16)
                sp.dma_start(K.vecs[:, :], ins["vecs"]).then_inc(stored, 16)
                sp.wait_ge(stored, 48)
        for stage in stages:
            stage(K)
        with nc.Block() as block:
            @block.sync
            def _(sp):
                src = K.X[:, :, :] if dump is None else dump(K)
                sp.dma_start(out, src).then_inc(stored, 16)
                sp.wait_ge(stored, 64)


def stage_norm(which):
    def run(K):
        norm(K, K.X, K.H, K.v(which))
    return run


def stage_final(which):
    def run(K):
        norm(K, K.X, K.H, K.v(which))
        K.X, K.H = K.H, K.X
    return run


def program(nc, ins, out, ntiles):
    build(nc, ins, out, [
        stage_norm("norm_mix0"), even_mixer, stage_norm("norm_mlp0"), lambda K: mlp(K, 0), lambda K: ple(K, 0),
        stage_norm("norm_mix1"), fox, stage_norm("norm_mlp1"), lambda K: mlp(K, 1), lambda K: ple(K, 1),
        stage_final("norm_final"),
        hgrn_layer, conv_layer, stage_final("norm_final2"),
        stage_norm("e_norm"), sgu_layer, stage_norm("o_norm"), rwkv_layer, stage_final("norm_final3")], ntiles)


def host_arrays(a):
    tiles = tiles_even(a) + tiles_mlp(a, 0) + tiles_ple(a, 0) + tiles_fox(a) + tiles_mlp(a, 1) + tiles_ple(a, 1) + \
        tiles_hgrn(a) + tiles_conv(a) + tiles_sgu(a) + tiles_rwkv(a)
    t = np.arange(T)[None, :]
    dft, dft_d = dft_tables()
    features_first = lambda x: x.T.reshape(-1, P, x.shape[0]).transpose(1, 0, 2)
    lora = lambda w: w.transpose(1, 0, 2).reshape(64, 2 * D)
    arrays = {
        "xT": features_first(a["x"][0]), "weights": np.stack(tiles), "vecs": host_vecs(a),
        "const": np.concatenate([v * np.ones((P, 1)) for v in const_tables().values()], axis=1).astype(np.float32),
        "pT": np.stack([features_first(a["p"][i, 0]) for i in range(2)]),
        "pos": a["positions"].reshape(1, T),
        "ctxT": features_first(a["ctx_2"][0]), "wv": values_hgrn(a),
        "sgu_w": a["e_sgu_w_3"][0].transpose(2, 0, 1), "sgu_b": a["e_sgu_b_3"].reshape(1, D),
        "sgu_ln_g": a["e_sgu_ln_g_3"].reshape(1, D), "sgu_ln_b": a["e_sgu_ln_b_3"].reshape(1, D),
        "dft": dft, "dft_d": dft_d, "fnet_w": a["o_fnet_w_3"][0].transpose(1, 0, 2),
        "w2a2": np.concatenate([lora(a["o_w2_3"][0]), lora(a["o_a2_3"][0])]),
        "resets64": np.broadcast_to(np.concatenate([t % 64 != 0, t % 64 != 63], axis=1), (P, 2 * T)).astype(np.float32),
    }
    return {k: np.ascontiguousarray(v) for k, v in arrays.items()}


def kernel(**inputs):
    import numpy as _np
    import concourse.bacc as _bacc
    from concourse import mybir as _mybir
    from concourse.bass_utils import run_bass_kernel_spmd as _run

    arrays = {"in_" + k: v for k, v in host_arrays({k: _np.asarray(v) for k, v in inputs.items()}).items()}
    nc = _bacc.Bacc("TRN2", target_bir_lowering=False, num_devices=1)
    ins = {k[3:]: nc.dram_tensor(k, v.shape, _mybir.dt.from_np(v.dtype), kind="ExternalInput").ap()
           for k, v in arrays.items()}
    out = nc.dram_tensor("out", (P, KD, T), _mybir.dt.float32, kind="ExternalOutput").ap()
    program(nc, ins, out, arrays["in_weights"].shape[0])
    r = _run(nc, [arrays], core_ids=[0])
    y = _np.asarray(r.results[0]["out"])
    return _np.ascontiguousarray(y.transpose(2, 1, 0)).reshape(1, T, D)
```
